# Optimizing a Trainium2 kernel written in Bass

```python
import math
import jax, jax.numpy as jnp
from jax import lax
import numpy as np

D_MODEL = 1024
BATCH = 1
SEQ = 512
DEPTH = 2

GLA_HEADS = 4
GLA_DK = 64
GLA_DV = 128
GLA_GATE_RANK = 16
GLA_GATE_TAU = 16.0
GLA_CHUNK = 64
ATT_HEADS = 8
ATT_HD = 64
DILATED_BRANCHES = ((128, 1), (512, 4), (2048, 16))
GLA_QK_W = GLA_HEADS * GLA_DK
GLA_V_W = GLA_HEADS * GLA_DV
ATT_W = ATT_HEADS * ATT_HD
AB_IN_W = 2 * GLA_QK_W + 2 * GLA_V_W + GLA_GATE_RANK + 3 * ATT_W
AB_OUT_W = GLA_V_W + ATT_W
D_RNN = 1024
RNN_BLOCKS = 8
RNN_BLOCK_W = D_RNN // RNN_BLOCKS
CONV_W = 4
LRU_C = 8.0
PEER_HEADS = 8
PEER_NKEYS = 128
PEER_EXPERTS = PEER_NKEYS * PEER_NKEYS
PEER_DQ = 256
PEER_TOPK = 16
PEER_BLOCK = 128
NORM_EPS = 1e-6
N_EVEN = (DEPTH + 1) // 2
N_ODD = DEPTH // 2

kernel_name = "hybrid_gla_dilated_rglru_peer"

def rms_norm(x, gain):
    xf = x.astype(jnp.float32)
    y = xf * lax.rsqrt(jnp.mean(xf * xf, axis=-1, keepdims=True) + NORM_EPS)
    return (y * gain.astype(jnp.float32)).astype(x.dtype)

def alibi_slopes(n):
    return 2.0 ** (-8.0 * jnp.arange(1, n + 1, dtype=jnp.float32) / n)

def gla_chunked(q, k, v, log_a):
    f32 = jnp.float32
    B, T, H, DK = q.shape
    DV = v.shape[-1]
    C = GLA_CHUNK
    N = T // C
    q = q.astype(f32).reshape(B, N, C, H, DK) * (DK ** -0.5)
    k = k.astype(f32).reshape(B, N, C, H, DK)
    v = v.astype(f32).reshape(B, N, C, H, DV)
    b = jnp.cumsum(log_a.astype(f32).reshape(B, N, C, H, DK), axis=2)
    b_last = b[:, :, -1]
    q_dec = q * jnp.exp(b)
    k_inv = k * jnp.exp(-b)
    causal = jnp.tril(jnp.ones((C, C), dtype=bool))
    att = jnp.where(causal, jnp.einsum('bnihk,bnjhk->bnhij', q_dec, k_inv), 0.0)
    o_intra = jnp.einsum('bnhij,bnjhv->bnihv', att, v)
    k_to_end = k * jnp.exp(b_last[:, :, None] - b)
    chunk_kv = jnp.einsum('bnjhk,bnjhv->bnhkv', k_to_end, v)

    def step(state, inp):
        decay, kv = inp
        return decay[..., None] * state + kv, state

    s0 = jnp.zeros((B, H, DK, DV), f32)
    _, s_prev = lax.scan(step, s0, (jnp.moveaxis(jnp.exp(b_last), 1, 0), jnp.moveaxis(chunk_kv, 1, 0)))
    s_prev = jnp.moveaxis(s_prev, 0, 1)
    o_inter = jnp.einsum('bnihk,bnhkv->bnihv', q_dec, s_prev)
    return (o_intra + o_inter).reshape(B, T, H, DV)

def strided_window_attention(q, k, v, n_sub, dilation, slopes):
    f32 = jnp.float32
    B, T, H, hd = q.shape
    L = T // dilation

    def to_sub(x):
        return x.reshape(B, L, dilation, H, hd).transpose(0, 2, 1, 3, 4).reshape(B * dilation, L, H, hd)

    def from_sub(x):
        rest = x.shape[2:]
        return x.reshape(B, dilation, L, *rest).swapaxes(1, 2).reshape(B, T, *rest)

    blk = n_sub
    nb = -(-L // blk)
    lp = nb * blk
    nn = B * dilation
    pad = ((0, 0), (0, lp - L), (0, 0), (0, 0))
    qs = jnp.pad(to_sub(q), pad)
    ks = jnp.pad(to_sub(k), pad)
    vs = jnp.pad(to_sub(v), pad)
    qb = qs.reshape(nn, nb, blk, H, hd)

    def with_prev(x):
        xp = jnp.pad(x, ((0, 0), (blk, 0), (0, 0), (0, 0)))
        prev = xp[:, :lp].reshape(nn, nb, blk, H, hd)
        cur = x.reshape(nn, nb, blk, H, hd)
        return jnp.concatenate([prev, cur], axis=2)

    kb, vb = with_prev(ks), with_prev(vs)
    s = jnp.einsum('nbqhd,nbkhd->nbhqk', qb, kb).astype(f32) * (hd ** -0.5)
    qi = jnp.arange(blk)[:, None]
    kj = jnp.arange(2 * blk)[None, :]
    delta = qi + blk - kj
    in_band = (delta >= 0) & (delta <= n_sub)
    not_front = (jnp.arange(nb)[:, None, None] > 0) | (kj >= blk)[None]
    valid = in_band[None] & not_front
    bias = -slopes[:, None, None] * (delta * dilation).astype(f32)
    s = jnp.where(valid[None, :, None], s + bias[None, None], -1e30)
    lse = jax.nn.logsumexp(s, axis=-1)
    p = jnp.exp(s - lse[..., None])
    o = jnp.einsum('nbhqk,nbkhd->nbqhd', p, vb.astype(f32)).reshape(nn, lp, H, hd)[:, :L]
    lse = jnp.moveaxis(lse, 2, 3).reshape(nn, lp, H)[:, :L]
    return from_sub(o), from_sub(lse)

def dilated_mixture_attention(q, k, v):
    slopes = alibi_slopes(ATT_HEADS)
    outs, lses = [], []
    for window, dil in DILATED_BRANCHES:
        o, l = strided_window_attention(q, k, v, window // dil, dil, slopes)
        outs.append(o)
        lses.append(l)
    w = jax.nn.softmax(jnp.stack(lses, axis=0), axis=0)
    return jnp.sum(w[..., None] * jnp.stack(outs, axis=0), axis=0)

def gla_dilated_mixer(h, w_in, w_alpha, b_alpha, head_gain, w_out):
    B, T, _ = h.shape
    f32 = jnp.float32
    proj = h @ w_in
    sizes = [GLA_QK_W, GLA_QK_W, GLA_V_W, GLA_V_W, GLA_GATE_RANK, ATT_W, ATT_W, ATT_W]
    splits = np.cumsum(sizes)[:-1].tolist()
    gq, gk, gv, gg, glr, aq, ak, av = jnp.split(proj, splits, axis=-1)
    log_a = jax.nn.log_sigmoid((glr @ w_alpha + b_alpha).astype(f32)) / GLA_GATE_TAU
    o_gla = gla_chunked(gq.reshape(B, T, GLA_HEADS, GLA_DK), gk.reshape(B, T, GLA_HEADS, GLA_DK),
                        gv.reshape(B, T, GLA_HEADS, GLA_DV), log_a.reshape(B, T, GLA_HEADS, GLA_DK))
    o_gla = o_gla * lax.rsqrt(jnp.mean(o_gla * o_gla, axis=-1, keepdims=True) + NORM_EPS)
    o_gla = o_gla.reshape(B, T, GLA_V_W) * head_gain.astype(f32) * jax.nn.silu(gg.astype(f32))
    o_att = dilated_mixture_attention(aq.reshape(B, T, ATT_HEADS, ATT_HD), ak.reshape(B, T, ATT_HEADS, ATT_HD),
                                      av.reshape(B, T, ATT_HEADS, ATT_HD)).reshape(B, T, ATT_W)
    mixed = jnp.concatenate([o_gla, o_att], axis=-1).astype(h.dtype)
    return mixed @ w_out

def rglru_mixer(h, w_in, conv_w, conv_b, w_rgate, b_rgate, w_igate, b_igate, lam, w_out):
    B, T, _ = h.shape
    f32 = jnp.float32
    proj = h @ w_in
    gate, xr = jnp.split(proj, 2, axis=-1)
    xc = lax.conv_general_dilated(xr, conv_w[:, None, :], window_strides=(1,), padding=[(CONV_W - 1, 0)],
                                  dimension_numbers=('NWC', 'WIO', 'NWC'), feature_group_count=D_RNN) + conv_b
    xb = xc.reshape(B, T, RNN_BLOCKS, RNN_BLOCK_W)
    r = jax.nn.sigmoid(jnp.einsum('btgi,gij->btgj', xb, w_rgate).reshape(B, T, D_RNN) + b_rgate)
    i = jax.nn.sigmoid(jnp.einsum('btgi,gij->btgj', xb, w_igate).reshape(B, T, D_RNN) + b_igate)
    log_a = -LRU_C * r.astype(f32) * jax.nn.softplus(-lam.astype(f32))
    a = jnp.exp(log_a)
    u = jnp.sqrt(-jnp.expm1(2.0 * log_a)) * (i * xc).astype(f32)

    def combine(left, right):
        a1, b1 = left
        a2, b2 = right
        return a1 * a2, a2 * b1 + b2

    _, hs = lax.associative_scan(combine, (a, u), axis=1)
    y = (jax.nn.gelu(gate.astype(f32)) * hs).astype(h.dtype)
    return y @ w_out

def peer_ffn(h, w_query, sub_keys, u_tab, v_tab):
    B, T, D = h.shape
    f32 = jnp.float32
    M = B * T
    K = PEER_TOPK
    H = PEER_HEADS
    hf = h.reshape(M, D)
    q = (hf @ w_query).reshape(M, H, 2, PEER_DQ // 2).astype(f32)
    s = jnp.einsum('mhpc,hpnc->mhpn', q, sub_keys.astype(f32))
    top_s, top_i = lax.top_k(s, K)
    cand_s = top_s[:, :, 0, :, None] + top_s[:, :, 1, None, :]
    cand_i = top_i[:, :, 0, :, None] * PEER_NKEYS + top_i[:, :, 1, None, :]
    best_s, best_c = lax.top_k(cand_s.reshape(M, H, K * K), K)
    ids = jnp.take_along_axis(cand_i.reshape(M, H, K * K), best_c, axis=-1)
    g = jax.nn.softmax(best_s, axis=-1)
    nblk = M // PEER_BLOCK
    ids = ids.reshape(nblk, PEER_BLOCK, H * K)
    g = g.reshape(nblk, PEER_BLOCK, H * K)
    hb = hf.reshape(nblk, PEER_BLOCK, D)

    def block(args):
        xb, idb, gb = args
        u = jnp.take(u_tab, idb, axis=0)
        v = jnp.take(v_tab, idb, axis=0)
        act = jax.nn.gelu(jnp.einsum('nkd,nd->nk', u, xb).astype(f32)) * gb
        return jnp.einsum('nk,nkd->nd', act.astype(v.dtype), v)

    out = lax.map(block, (hb, ids, g))
    return out.reshape(B, T, D).astype(h.dtype)

def setup_inputs(seed: int = 0) -> dict:
    key = jax.random.key(seed)
    ks = jax.random.split(key, 24)
    nrm = jax.random.normal
    D = D_MODEL
    lru_u = jax.random.uniform(ks[14], (N_ODD, D_RNN), minval=0.9, maxval=0.999)
    lru_a = lru_u ** (1.0 / LRU_C)
    return {
        "x": nrm(ks[0], (BATCH, SEQ, D), jnp.float32),
        "mix_norm": 1.0 + 0.02 * nrm(ks[1], (DEPTH, D)),
        "ffn_norm": 1.0 + 0.02 * nrm(ks[2], (DEPTH, D)),
        "ab_w_in": nrm(ks[3], (N_EVEN, D, AB_IN_W)) * D ** -0.5,
        "gla_w_alpha": nrm(ks[4], (N_EVEN, GLA_GATE_RANK, GLA_QK_W)) * GLA_GATE_RANK ** -0.5,
        "gla_b_alpha": 0.1 * nrm(ks[5], (N_EVEN, GLA_QK_W)),
        "gla_head_gain": 1.0 + 0.02 * nrm(ks[6], (N_EVEN, GLA_V_W)),
        "ab_w_out": nrm(ks[7], (N_EVEN, AB_OUT_W, D)) * AB_OUT_W ** -0.5,
        "c_w_in": nrm(ks[8], (N_ODD, D, 2 * D_RNN)) * D ** -0.5,
        "c_conv_w": nrm(ks[9], (N_ODD, CONV_W, D_RNN)) * CONV_W ** -0.5,
        "c_conv_b": 0.02 * nrm(ks[10], (N_ODD, D_RNN)),
        "c_w_rgate": nrm(ks[11], (N_ODD, RNN_BLOCKS, RNN_BLOCK_W, RNN_BLOCK_W)) * RNN_BLOCK_W ** -0.5,
        "c_b_rgate": 0.02 * nrm(ks[12], (N_ODD, D_RNN)),
        "c_w_igate": nrm(ks[13], (N_ODD, RNN_BLOCKS, RNN_BLOCK_W, RNN_BLOCK_W)) * RNN_BLOCK_W ** -0.5,
        "c_b_igate": 0.02 * nrm(ks[15], (N_ODD, D_RNN)),
        "c_lambda": jnp.log(lru_a) - jnp.log1p(-lru_a),
        "c_w_out": nrm(ks[16], (N_ODD, D_RNN, D)) * D_RNN ** -0.5,
        "peer_w_query": nrm(ks[17], (DEPTH, D, PEER_HEADS * PEER_DQ)) * D ** -0.5,
        "peer_sub_keys": nrm(ks[18], (DEPTH, PEER_HEADS, 2, PEER_NKEYS, PEER_DQ // 2)) * (PEER_DQ // 2) ** -0.5,
        "peer_u": nrm(ks[19], (DEPTH, PEER_EXPERTS, D)) * D ** -0.5,
        "peer_v": nrm(ks[20], (DEPTH, PEER_EXPERTS, D)) * (PEER_HEADS * PEER_TOPK) ** -0.5,
        "final_norm": 1.0 + 0.02 * nrm(ks[21], (D,)),
    }

def reference(x, mix_norm, ffn_norm, ab_w_in, gla_w_alpha, gla_b_alpha, gla_head_gain, ab_w_out,
              c_w_in, c_conv_w, c_conv_b, c_w_rgate, c_b_rgate, c_w_igate, c_b_igate, c_lambda, c_w_out,
              peer_w_query, peer_sub_keys, peer_u, peer_v, final_norm):
    h = x
    for layer in range(DEPTH):
        hn = rms_norm(h, mix_norm[layer])
        if layer % 2 == 0:
            e = layer // 2
            h = h + gla_dilated_mixer(hn, ab_w_in[e], gla_w_alpha[e], gla_b_alpha[e], gla_head_gain[e], ab_w_out[e])
        else:
            o = layer // 2
            h = h + rglru_mixer(hn, c_w_in[o], c_conv_w[o], c_conv_b[o], c_w_rgate[o], c_b_rgate[o],
                                c_w_igate[o], c_b_igate[o], c_lambda[o], c_w_out[o])
        hn = rms_norm(h, ffn_norm[layer])
        h = h + peer_ffn(hn, peer_w_query[layer], peer_sub_keys[layer], peer_u[layer], peer_v[layer])
    return rms_norm(h, final_norm)


_drawn_inputs = setup_inputs


def setup_inputs(seed=0):
    import zlib

    import numpy as np

    out = dict(_drawn_inputs(seed))
    spreads = {}
    factors = {'ffn_norm': 6.536,
     'gla_b_alpha': 2.842,
     'gla_head_gain': 5.704,
     'c_b_rgate': 64.0,
     'c_b_igate': 39.407,
     'final_norm': 7.54}
    for name, (base, spread) in spreads.items():
        noise = np.random.default_rng([zlib.crc32(name.encode()), seed]).standard_normal(out[name].shape)
        drawn = base * np.exp(spread * noise) if base else spread * noise
        out[name] = __import__('jax').numpy.asarray(drawn.astype(out[name].dtype))
    for name, factor in factors.items():
        out[name] = (out[name] * factor).astype(out[name].dtype)
    return out
```

```python
import math
from contextlib import ExitStack

import numpy as np

import concourse.bass as bass
from concourse import mybir

F32 = mybir.dt.float32
F32R = mybir.dt.float32r
I32 = mybir.dt.int32
U32 = mybir.dt.uint32
ALU = mybir.AluOpType
ACT = mybir.ActivationFunctionType
AX = mybir.AxisListType

P = 128
D = 1024
KD = D // P
T = 512
NT = T // P
EPS = 1e-6
BC = 256

GH, GDK, GDV, GRANK, GCHUNK = 4, 64, 128, 16, 64
GPAIRS = GH * GDK // P
GV_W = GH * GDV
NCHUNK = T // GCHUNK
GATE_TAU = 16.0
AH, AHD = 8, 64
BRANCHES = ((128, 1), (512, 4), (2048, 16))
RT = D // P
CONV = 4
LRU_C = 8.0
PH, PK, NKEYS = 8, 16, 128
HK = PH * PK
NEXP = NKEYS * NKEYS
NCH = NEXP // P
SPAN = 8
TB = 32
NEG = -3.0e38
CAND = []
_at = 0
for _a0, _na in ((0, 1), (1, 1), (2, 1), (3, 1), (4, 1), (5, 3), (8, 8)):
    CAND.append((_a0, _na, PK // (_a0 + 1), _at))
    _at += _na * (PK // (_a0 + 1))
NCAND = _at


def wait(eng, sem, value):
    if not (isinstance(value, int) and value <= 0):
        eng.wait_ge(sem, value)


class Scope:

    HELD = []

    @classmethod
    def reset(cls, nc):
        nc.clear_and_free_semaphores(list(cls.HELD))
        nc.all_engine_barrier()
        cls.HELD.clear()

    def __init__(self, nc, name):
        self.nc, self.name, self.stack = nc, name, ExitStack()

    def __enter__(self):
        self.stack.__enter__()
        return self

    def __exit__(self, *a):
        return self.stack.__exit__(*a)

    def sb(self, name, shape, dt=F32):
        return self.stack.enter_context(self.nc.sbuf_tensor(f"{self.name}_{name}", shape, dt))

    def ps(self, name, shape):
        return self.stack.enter_context(self.nc.psum_tensor(f"{self.name}_{name}", shape, F32))

    def sem(self, name):
        held = self.nc.alloc_semaphore(f"{self.name}_{name}")
        self.HELD.append(held)
        return held

    def block(self):
        return self.stack.enter_context(self.nc.Block())


class Chain:

    def __init__(self, eng, sem, start=0):
        self.eng, self.sem, self.n = eng, sem, start

    def link(self, ins):
        self.n = self.n + 1
        ins.then_inc(self.sem, 1)
        self.eng.wait_ge(self.sem, self.n)


def norm_stage(nc, name, resid, gain, ident, xh, xl):
    with Scope(nc, name) as s:
        xn = s.sb("xn", [P, NT, D])
        ss = s.sb("ss", [P, NT])
        ms = s.sb("ms", [P, NT])
        root = s.sb("root", [P, NT])
        rs = s.sb("rs", [P, NT])
        ps = s.ps("ps", [P, KD, T])
        squared, mean, rooted, chain = s.sem("squared"), s.sem("mean"), s.sem("rooted"), s.sem("chain")
        normed, turned, hi = s.sem("normed"), s.sem("turned"), s.sem("hi")
        block = s.block()

        @block.scalar
        def _(act):
            for t in range(NT):
                nc.scalar.activation(xn[:, t], resid[:, t], ACT.Square, accum_out=ss[:, t:t + 1]).then_inc(squared, 1)
            act.wait_ge(mean, 1)
            nc.scalar.activation(root[:], ms[:], ACT.Sqrt).then_inc(rooted, 1)
            for c in range(KD):
                act.wait_ge(turned, c + 1)
                nc.scalar.activation(xh[:, c], ps[:, c], ACT.Copy, scale=gain[:, c:c + 1]).then_inc(hi, 1)

        @block.vector
        def _(dve):
            ch = Chain(dve, chain)
            dve.wait_ge(squared, NT)
            nc.vector.tensor_scalar(ms[:], ss[:], 1.0 / D, EPS, ALU.mult, ALU.add).then_inc(mean, 1)
            dve.wait_ge(rooted, 1)
            ch.link(nc.vector.reciprocal(rs[:], root[:]))
            for t in range(NT):
                nc.vector.tensor_scalar(xn[:, t], resid[:, t], rs[:, t:t + 1], None, ALU.mult).then_inc(normed, 1)
            for c in range(KD):
                dve.wait_ge(hi, c + 1)
                nc.vector.scalar_tensor_tensor(xl[:, c], ps[:, c], gain[:, c:c + 1], xh[:, c].bitcast(F32),
                                               ALU.mult, ALU.subtract)

        @block.tensor
        def _(pe):
            for t in range(NT):
                pe.wait_ge(normed, t + 1)
                for c in range(KD):
                    last = nc.tensor.transpose(ps[:, c, t * P:(t + 1) * P], xn[:, t, c * P:(c + 1) * P], ident[:])
                    if t == NT - 1:
                        last.then_inc(turned, 1)


class Weights:

    def __init__(self, nc, s, dram, count):
        self.nc, self.dram, self.count = nc, dram, count
        self.raw = s.sb("w_raw", [P, 2, KD, BC])
        self.wh = s.sb("w_hi", [P, 2, KD, BC], F32R)
        self.wl = s.sb("w_lo", [P, 2, KD, BC], F32R)
        self.loaded = [s.sem(f"w_loaded{k}") for k in range(2)]
        self.high, self.low, self.used = s.sem("w_high"), s.sem("w_low"), s.sem("products_done")

    def load(self, sp, r, k):
        n = r * 2 + k
        wait(sp, self.low, n - 1)
        sp.dma_start(self.raw[:, k].rearrange("p k c -> p (k c)"), self.dram[n]).then_inc(self.loaded[k], 16)

    def split_high(self, act, r, k):
        act.wait_ge(self.loaded[k], r * 16 + 16)
        wait(act, self.used, (r * 2 + k) - 1)
        self.nc.scalar.activation(self.wh[:, k], self.raw[:, k], ACT.Copy).then_inc(self.high, 1)

    def split_low(self, pool, r, k):
        pool.wait_ge(self.high, r * 2 + k + 1)
        self.nc.gpsimd.tensor_tensor(self.wl[:, k], self.raw[:, k], self.wh[:, k].bitcast(F32),
                                     ALU.subtract).then_inc(self.low, 1)

    def rounds(self, eng, body):
        body(0)
        if self.count > 2:
            with eng.Fori(1, self.count // 2) as r:
                body(r)


def three_pass(nc, out, lh, ll, rh, rl, first, last):
    nc.tensor.matmul(out, lh, rh, start=first, stop=False)
    nc.tensor.matmul(out, lh, rl, start=False, stop=False)
    return nc.tensor.matmul(out, ll, rh, start=False, stop=last)


def block_products(nc, w, k, xh, xl, ps, by_column):
    if by_column:
        for c in range(2):
            for d in range(KD):
                cs = slice(c * P, (c + 1) * P)
                last = three_pass(nc, ps[:, k, c], w.wh[:, k, d, cs], w.wl[:, k, d, cs], xh[:, d], xl[:, d],
                                  d == 0, d == KD - 1)
    else:
        for t in range(NT):
            ts, half = slice(t * P, (t + 1) * P), slice((t % 2) * BC, (t % 2 + 1) * BC)
            for d in range(KD):
                last = three_pass(nc, ps[:, k, t // 2, half], xh[:, d, ts], xl[:, d, ts], w.wh[:, k, d], w.wl[:, k, d],
                                  d == 0, d == KD - 1)
    return last


def project_stage(nc, name, dram, count, xh, xl, dest, by_column, add=False):
    with Scope(nc, name) as s:
        w = Weights(nc, s, dram, count)
        ps = s.ps("ps", [P, 2, 2, T])
        done = w.used
        taken = s.sem("out_taken")
        block = s.block()

        @block.sync
        def _(sp):
            w.rounds(sp, lambda r: [w.load(sp, r, k) for k in range(2)])

        @block.gpsimd
        def _(pool):
            w.rounds(pool, lambda r: [w.split_low(pool, r, k) for k in range(2)])

        @block.scalar
        def _(act):
            w.rounds(act, lambda r: [w.split_high(act, r, k) for k in range(2)])

        @block.vector
        def _(dve):
            def body(r):
                for k in range(2):
                    dve.wait_ge(done, r * 2 + k + 1)
                    n = r * 2 + k
                    if by_column:
                        out = dest[:, bass.ds(n * 2, 2)]
                        nc.vector.tensor_copy(out, ps[:, k]).then_inc(taken, 1)
                    else:
                        out = dest[:, :, bass.ds(n * BC, BC)]
                        src = ps[:, k].rearrange("p a (b c) -> p (a b) c", b=2)
                        if add:
                            nc.vector.tensor_tensor(out, src, out, ALU.add).then_inc(taken, 1)
                        else:
                            nc.vector.tensor_copy(out, src).then_inc(taken, 1)
            w.rounds(dve, body)

        @block.tensor
        def _(pe):
            def body(r):
                for k in range(2):
                    pe.wait_ge(w.low, r * 2 + k + 1)
                    wait(pe, taken, (r * 2 + k) - 1)
                    block_products(nc, w, k, xh, xl, ps, by_column).then_inc(done, 1)
            w.rounds(pe, body)


def query_stage(nc, name, dram, keys_dram, xh, xl, scores):
    with Scope(nc, name) as s:
        w = Weights(nc, s, dram, PH)
        keys = s.sb("keys", [P, 2 * PH * NKEYS])
        q = s.sb("q", [P, 2, 2, T])
        ps = s.ps("ps", [P, 2, 2, T])
        ps_s = s.ps("ps_s", [P, 2, NT, NKEYS])
        done = w.used
        keys_in, q_there, s_done, s_taken = s.sem("keys_in"), s.sem("q_there"), s.sem("s_done"), s.sem("s_taken")
        block = s.block()

        @block.sync
        def _(sp):
            sp.dma_start(keys[:], keys_dram).then_inc(keys_in, 16)
            w.rounds(sp, lambda r: [w.load(sp, r, k) for k in range(2)])

        @block.gpsimd
        def _(pool):
            w.rounds(pool, lambda r: [w.split_low(pool, r, k) for k in range(2)])

        @block.scalar
        def _(act):
            w.rounds(act, lambda r: [w.split_high(act, r, k) for k in range(2)])

        @block.vector
        def _(dve):
            def take_scores(n):
                dve.wait_ge(s_done, n + 1)
                for p in range(2):
                    last = nc.vector.tensor_copy(scores[:, :, bass.ds(n * 2 + p, 1)].rearrange("p t o c -> p t (o c)"),
                                                 ps_s[:, p])
                last.then_inc(s_taken, 1)

            def body(r):
                for k in range(2):
                    dve.wait_ge(done, r * 2 + k + 1)
                    wait(dve, s_done, r * 2 + k - 1)
                    nc.vector.tensor_copy(q[:, k], ps[:, k]).then_inc(q_there, 1)
                    if not (isinstance(r, int) and k == 0):
                        take_scores(r * 2 + k - 1)
            w.rounds(dve, body)
            take_scores(PH - 1)

        @block.tensor
        def _(pe):
            def score(n, k):
                pe.wait_ge(q_there, n + 1)
                wait(pe, s_taken, n)
                for p in range(2):
                    kp = keys[:, bass.ds((n * 2 + p) * NKEYS, NKEYS)]
                    for t in range(NT):
                        last = nc.tensor.matmul(ps_s[:, p, t], q[:, k, p, t * P:(t + 1) * P], kp, start=True, stop=True)
                last.then_inc(s_done, 1)

            def body(r):
                for k in range(2):
                    pe.wait_ge(w.low, r * 2 + k + 1)
                    wait(pe, q_there, (r * 2 + k) - 1)
                    block_products(nc, w, k, xh, xl, ps, True).then_inc(done, 1)
                    if isinstance(r, int) and k == 0:
                        pe.wait_ge(keys_in, 16)
                    else:
                        score(r * 2 + k - 1, 1 - k)
            w.rounds(pe, body)
            score(PH - 1, 1)


def up_stage(nc, name, uT, h_dram, g_dram, consts, xh, xl, scores):
    ident, iota, cand_iota = consts["ident"], consts["iota"], consts["cand_iota"]
    SETS = NCH // SPAN
    PLAIN = SETS // 2
    TOK = 2 * TB
    BATCH = 4
    with Scope(nc, name) as s:
        raw = s.sb("u_raw", [P, 2, 2, KD, P])
        uh = s.sb("u_hi", [P, 2, KD, P], F32R)
        ul = s.sb("u_lo", [P, 2, KD, P], F32R)
        hs = s.sb("h_out", [P, 2, 2, T])
        gst = s.sb("g_out", [P, 2, NKEYS, TB])
        work = s.sb("work", [P, 2 * PH, NKEYS])
        top = s.sb("top", [P, 2 * PH, PK])
        topi = s.sb("topi", [P, 2 * PH, PK], U32)
        topf = s.sb("topf", [P, 2 * PH, PK])
        cv = s.sb("cv", [P, PH, NCAND])
        ci = s.sb("ci", [P, PH, NCAND])
        best = s.sb("best", [P, PH, PK])
        posi = s.sb("posi", [P, PH, PK], U32)
        posf = s.sb("posf", [P, PH, PK])
        pick = s.sb("pick", [P, PK, NCAND])
        idf = s.sb("idf", [P, HK])
        idi = s.sb("idi", [P, 3, HK], I32)
        ijg = s.sb("ijg", [P, 3, HK])
        ex = s.sb("ex", [P, PH, PK])
        tick = s.sb("tick", [P, 1])
        den = s.sb("den", [P, PH])
        ijgT = s.sb("ijgT", [P, 3, T])
        here = s.sb("here", [P, 3, TOK])
        ghi = s.sb("ghi", [P, TOK], F32R)
        glo = s.sb("glo", [P, TOK])
        oh = s.sb("onehot", [P, 2, BATCH, 3, P], F32R)
        ps_u = s.ps("ps_u", [P, 4, T])
        ps_t = s.ps("ps_t", [P, 3, P])
        ps_g = s.ps("ps_g", [P, 2, BATCH, NKEYS])

        loaded = [s.sem(f"u_loaded{k}") for k in range(2)]
        high, low, used = s.sem("u_high"), s.sem("u_low"), s.sem("u_used")
        h_there = s.sem("h_there")
        h_stored = [s.sem(f"h_stored{k}") for k in range(2)]
        chain, diff, exped = s.sem("choice_chain"), s.sem("diff"), s.sem("exped")
        chosen, turned, kept = s.sem("chosen"), s.sem("turned"), s.sem("kept")
        onehots, g_done, g_there = s.sem("onehots"), s.sem("g_done"), s.sem("g_there")
        g_stored = [s.sem(f"g_stored{k}") for k in range(2)]
        block = s.block()

        @block.sync
        def _(sp):
            def body(r, peeled, second):
                for q in range(SPAN // 2):
                    n, k = r * (SPAN // 2) + q, q % 2
                    if not (peeled and q < 2):
                        sp.wait_ge(low, n * 2 - 2)
                    sp.dma_start(raw[:, k].rearrange("p a k e -> p (a k e)"), uT[n]).then_inc(loaded[k], 16)
                    if not (peeled and q < 3):
                        m = n - 3
                        sp.wait_ge(h_there, m * 2 + 2)
                        sp.dma_start(h_dram[m], hs[:, (q + 1) % 2].rearrange("p a t -> p (a t)")).then_inc(
                            h_stored[(q + 1) % 2], 16)
                    if second is not None and q % 2 == 1:
                        b, kb = (second * 2 - 1, 1) if q == 1 else (second * 2, 0)
                        if not (isinstance(b, int) and b < 0):
                            sp.wait_ge(g_there, (b + 1) * (TB // BATCH))
                            sp.dma_start(g_dram[b], gst[:, kb].rearrange("p i t -> p (i t)")).then_inc(g_stored[kb], 16)
            body(0, True, None)
            with sp.Fori(1, PLAIN) as r:
                body(r, False, None)
            body(PLAIN, False, 0)
            with sp.Fori(1, SETS - PLAIN) as r:
                body(r + PLAIN, False, r)
            for m in range(NCH // 2 - 3, NCH // 2):
                sp.wait_ge(h_there, m * 2 + 2)
                sp.dma_start(h_dram[m], hs[:, m % 2].rearrange("p a t -> p (a t)")).then_inc(h_stored[m % 2], 16)
            b = T // TB - 1
            sp.wait_ge(g_there, T // BATCH)
            sp.dma_start(g_dram[b], gst[:, 1].rearrange("p i t -> p (i t)")).then_inc(g_stored[1], 16)
            for k in range(2):
                sp.wait_ge(h_stored[k], NCH // 4 * 16)
                sp.wait_ge(g_stored[k], T // TB // 2 * 16)

        @block.gpsimd
        def _(pool):
            def body(r, peeled):
                for q in range(SPAN):
                    n = r * SPAN + q
                    pool.wait_ge(high, n + 1)
                    nc.gpsimd.tensor_tensor(ul[:, q % 2], raw[:, q // 2 % 2, q % 2], uh[:, q % 2].bitcast(F32),
                                            ALU.subtract).then_inc(low, 1)
            with pool.Fori(0, SETS) as r:
                body(r, False)

        @block.scalar
        def _(act):
            def body(r, peeled, second, at_five=None):
                for q in range(SPAN):
                    n = r * SPAN + q
                    act.wait_ge(loaded[q // 2 % 2], r * (16 * SPAN // 4) + 16 * (q // 4 + 1))
                    if not (peeled and q < 2):
                        act.wait_ge(used, n - 1)
                    nc.scalar.activation(uh[:, q % 2], raw[:, q // 2 % 2, q % 2], ACT.Copy).then_inc(high, 1)
                    if not (peeled and q < 2):
                        after(r if q >= 2 else r - 1, (q - 2) % SPAN, second if q >= 2 or second is None else second - 1)
                    if q == 5 and at_five:
                        at_five()

            def after(r, q, second):
                n = r * SPAN + q
                act.wait_ge(used, n + 1)
                if q % 2 == 0 and not (isinstance(r, int) and r == 0 and q < 4):
                    act.wait_ge(h_stored[q // 2 % 2], r * (16 * SPAN // 4) + 16 * (q // 4))
                nc.scalar.activation(hs[:, q // 2 % 2, q % 2], ps_u[:, q % 4], ACT.Gelu_apprx_tanh).then_inc(h_there, 1)
                if second is None or (isinstance(second, int) and second < 0):
                    return
                for b in (2 * q, 2 * q + 1):
                    kb, t0 = b * BATCH // TB, b * BATCH % TB
                    act.wait_ge(g_done, second * (TOK // BATCH) + b + 1)
                    if t0 == 0 and not (isinstance(second, int) and second == 0):
                        act.wait_ge(g_stored[kb], second * 16)
                    nc.scalar.activation(gst[:, kb, :, t0:t0 + BATCH].rearrange("p i t -> p t i"), ps_g[:, b % 2],
                                         ACT.Copy).then_inc(g_there, 1)

            def exponentials(c):
                act.wait_ge(diff, c + 1)
                nc.scalar.activation(ex[:], best[:], ACT.Exp).then_inc(exped, 1)

            def keep(c):
                act.wait_ge(turned, c + 1)
                nc.scalar.activation(ijgT[:, :, bass.ds(c * P, P)], ps_t[:], ACT.Copy).then_inc(kept, 1)

            body(0, True, None)
            body(1, False, None, lambda: exponentials(0))
            keep(0)
            with act.Fori(1, NT) as c:
                body(c * 2, False, None)
                body(c * 2 + 1, False, None, lambda: exponentials(c))
                keep(c)
            body(PLAIN, False, 0)
            with act.Fori(1, SETS - PLAIN) as r:
                body(r + PLAIN, False, r)
            for q in (SPAN - 2, SPAN - 1):
                after(SETS - 1, q, SETS - PLAIN - 1)

        @block.vector
        def _(dve):
            LINKS = 44

            def choose(c):
                links = [0]

                def link(ins):
                    links[0] += 1
                    ins.then_inc(chain, 1)
                    dve.wait_ge(chain, c * LINKS + links[0])
                    nc.vector.memset(tick[:], 0.0)

                link(nc.vector.tensor_copy(work[:], scores[:, bass.ds(c, 1)].rearrange("p o a n -> p (o a) n")))
                for v in range(2):
                    e = slice(8 * v, 8 * v + 8)
                    for a in range(2 * PH):
                        last = nc.vector.max(top[:, a, e], work[:, a])
                    link(last)
                    for a in range(2 * PH):
                        last = nc.vector.max_index(topi[:, a, e], top[:, a, e], work[:, a])
                    link(last)
                    if v == 0:
                        for a in range(2 * PH):
                            last = nc.vector.match_replace(work[:, a], top[:, a, e], work[:, a], NEG)
                        link(last)
                link(nc.vector.tensor_copy(topf[:], topi[:]))
                tf = topf[:].rearrange("p (h o) k -> p h o k", o=2)
                tv = top[:].rearrange("p (h o) k -> p h o k", o=2)
                link(nc.vector.tensor_scalar(tf[:, :, 0], tf[:, :, 0], float(NKEYS), None, ALU.mult))
                for src, dst in ((tv, cv), (tf, ci)):
                    for a0, na, nb, at in CAND:
                        out = dst[:, :, at:at + na * nb].rearrange("p h (a b) -> p h a b", a=na)
                        one = src[:, :, 0, a0:a0 + na].unsqueeze(3).to_broadcast([P, PH, na, nb])
                        two = src[:, :, 1, 0:nb].unsqueeze(2).to_broadcast([P, PH, na, nb])
                        last = nc.vector.tensor_tensor(out, one, two, ALU.add)
                link(last)
                for v in range(2):
                    e = slice(8 * v, 8 * v + 8)
                    for h in range(PH):
                        last = nc.vector.max(best[:, h, e], cv[:, h])
                    link(last)
                    for h in range(PH):
                        last = nc.vector.max_index(posi[:, h, e], best[:, h, e], cv[:, h])
                    link(last)
                    if v == 0:
                        for h in range(PH):
                            last = nc.vector.match_replace(cv[:, h], best[:, h, e], cv[:, h], NEG)
                        link(last)
                link(nc.vector.tensor_copy(posf[:], posi[:]))
                for h in range(PH):
                    pos = posf[:, h].unsqueeze(2).to_broadcast([P, PK, NCAND])
                    cio = cand_iota[:].unsqueeze(1).to_broadcast([P, PK, NCAND])
                    cih = ci[:, h].unsqueeze(1).to_broadcast([P, PK, NCAND])
                    link(nc.vector.tensor_tensor(pick[:], pos, cio, ALU.is_equal))
                    link(nc.vector.tensor_tensor(pick[:], pick[:], cih, ALU.mult))
                    link(nc.vector.tensor_reduce(idf[:, h * PK:(h + 1) * PK], pick[:], AX.X, ALU.add))
                first = best[:, :, 0:1].to_broadcast([P, PH, PK - 1])
                link(nc.vector.tensor_tensor(best[:, :, 1:], best[:, :, 1:], first, ALU.subtract))
                nc.vector.memset(best[:, :, 0:1], 0.0).then_inc(diff, 1)
                dve.wait_ge(exped, c + 1)
                link(nc.vector.tensor_reduce(den[:], ex[:], AX.X, ALU.add))
                link(nc.vector.reciprocal(den[:], den[:]))
                if not isinstance(c, int):
                    dve.wait_ge(turned, c)
                nc.vector.tensor_tensor(ijg[:, 2].rearrange("p (h k) -> p h k", h=PH), ex[:],
                                        den[:].unsqueeze(2).to_broadcast([P, PH, PK]), ALU.mult)
                link(nc.vector.tensor_copy(idi[:, 0], idf[:]))
                nc.vector.tensor_scalar(idi[:, 1], idi[:, 0], 7, None, ALU.arith_shift_right)
                link(nc.vector.tensor_scalar(idi[:, 2], idi[:, 0], NKEYS - 1, None, ALU.bitwise_and))
                nc.vector.tensor_copy(ijg[:, 0:2], idi[:, 1:3]).then_inc(chosen, 1)
                assert links[0] == LINKS, links[0]

            def gates(second):
                L = 3
                dve.wait_ge(kept, NT)
                if not isinstance(second, int):
                    dve.wait_ge(onehots, second * (TOK // BATCH))
                base = NT * LINKS
                nc.vector.tensor_copy(here[:], ijgT[:, :, bass.ds(second * TOK, TOK)]).then_inc(chain, 1)
                dve.wait_ge(chain, second * L + base + 1)
                nc.vector.tensor_copy(ghi[:], here[:, 2]).then_inc(chain, 1)
                dve.wait_ge(chain, second * L + base + 2)
                nc.vector.tensor_tensor(glo[:], here[:, 2], ghi[:].bitcast(F32), ALU.subtract).then_inc(chain, 1)
                dve.wait_ge(chain, second * L + base + 3)
                for b in range(TOK // BATCH):
                    if not (isinstance(second, int) and b < 2):
                        dve.wait_ge(g_done, second * (TOK // BATCH) + b - 1)
                    for t in range(BATCH):
                        o, tok = oh[:, b % 2, t], b * BATCH + t
                        ti, tj = here[:, 0, tok:tok + 1], here[:, 1, tok:tok + 1]
                        nc.vector.tensor_scalar(o[:, 0], iota[:], tj, None, ALU.is_equal)
                        nc.vector.tensor_scalar(o[:, 1], iota[:], ti, ghi[:, tok:tok + 1].bitcast(F32), ALU.is_equal, ALU.mult)
                        last = nc.vector.tensor_scalar(o[:, 2], iota[:], ti, glo[:, tok:tok + 1], ALU.is_equal, ALU.mult)
                    last.then_inc(onehots, 1)

            choose(0)
            with dve.Fori(1, NT) as c:
                choose(c)
            gates(0)
            with dve.Fori(1, SETS - PLAIN) as r:
                gates(r)

        @block.tensor
        def _(pe):
            def body(r, peeled, second):
                for q in range(SPAN):
                    n = r * SPAN + q
                    pe.wait_ge(low, n + 1)
                    if not (peeled and q < 4):
                        pe.wait_ge(h_there, n - 3)
                    for d in range(KD):
                        last = three_pass(nc, ps_u[:, q % 4], uh[:, q % 2, d], ul[:, q % 2, d], xh[:, d], xl[:, d],
                                          d == 0, d == KD - 1)
                    last.then_inc(used, 1)
                    if second is not None:
                        for b in range(2):
                            gate(second, q * 2 + b)

            def gate(second, b):
                m = second * (TOK // BATCH) + b
                pe.wait_ge(onehots, m + 1)
                if not (isinstance(second, int) and b < 2):
                    pe.wait_ge(g_there, m - 1)
                for t in range(BATCH):
                    o = oh[:, b % 2, t]
                    nc.tensor.matmul(ps_g[:, b % 2, t], o[:, 0], o[:, 1], start=True, stop=False)
                    last = nc.tensor.matmul(ps_g[:, b % 2, t], o[:, 0], o[:, 2], start=False, stop=True)
                last.then_inc(g_done, 1)

            def turn(c):
                pe.wait_ge(chosen, c + 1)
                if not isinstance(c, int):
                    pe.wait_ge(kept, c)
                for v in range(3):
                    last = nc.tensor.transpose(ps_t[:, v], ijg[:, v], ident[:])
                last.then_inc(turned, 1)

            body(0, True, None)
            body(1, False, None)
            turn(0)
            with pe.Fori(1, NT) as c:
                body(c * 2, False, None)
                body(c * 2 + 1, False, None)
                turn(c)
            body(PLAIN, False, 0)
            with pe.Fori(1, SETS - PLAIN) as r:
                body(r + PLAIN, False, r)


def down_stage(nc, name, v, h_dram, g_dram, resid):
    SETS = NCH // SPAN
    QUAD = 4
    with Scope(nc, name) as s:
        raw = s.sb("v_raw", [P, 4, 2, D])
        vh = s.sb("v_hi", [P, 4, D], F32R)
        vl = s.sb("v_lo", [P, 4, D], F32R)
        hin = s.sb("h_in", [P, 4, 2, T])
        gin = s.sb("g_in", [P, 2, T // TB, QUAD, TB])
        a = s.sb("a", [P, 4, T])
        ah = s.sb("a_hi", [P, 4, T], F32R)
        al = s.sb("a_lo", [P, 4, T], F32R)
        ps = s.ps("ps", [P, NT, 2, T])
        v_in = [s.sem(f"v_in{k}") for k in range(4)]
        h_in = [s.sem(f"h_in{k}") for k in range(4)]
        g_in = [s.sem(f"g_in{k}") for k in range(2)]
        v_high, v_low, a_there, a_high, a_low, used = (s.sem("v_high"), s.sem("v_low"), s.sem("a_there"), s.sem("a_high"),
                                                      s.sem("a_low"), s.sem("used"))
        block = s.block()
        v_rows = v.rearrange("(n a j) d -> n j a d", a=2, j=P)
        h_rows = h_dram
        g_rows = g_dram.rearrange("b j x -> j b x")

        @block.sync
        def _(sp):
            def body(r, peeled):
                for q in range(SPAN // 2):
                    n = r * (SPAN // 2) + q
                    if q % 2 == 0:
                        kg = q // 2
                        if not peeled:
                            sp.wait_ge(a_there, r * SPAN - SPAN + QUAD * (kg + 1))
                        sp.dma_start(gin[:, kg].rearrange("p b i t -> p b (i t)"),
                                     g_rows[:, :, bass.ds(n * (2 * TB), QUAD * TB)]).then_inc(
                                         g_in[kg], 16)
                    if not peeled:
                        sp.wait_ge(a_there, r * SPAN - SPAN + 2 * (q + 1))
                    sp.dma_start(hin[:, q].rearrange("p a t -> p (a t)"), h_rows[n]).then_inc(h_in[q], 16)
                    if not peeled:
                        sp.wait_ge(v_low, r * SPAN - SPAN + 2 * (q + 1))
                    sp.dma_start(raw[:, q], v_rows[n]).then_inc(v_in[q], 16)
            body(0, True)
            with sp.Fori(1, SETS) as r:
                body(r, False)

        @block.gpsimd
        def _(pool):
            with pool.Fori(0, SETS) as r:
                for q in range(SPAN):
                    pool.wait_ge(v_high, r * SPAN + q + 1)
                    nc.gpsimd.tensor_tensor(vl[:, q % 4], raw[:, q // 2, q % 2], vh[:, q % 4].bitcast(F32),
                                            ALU.subtract).then_inc(v_low, 1)

        @block.scalar
        def _(act):
            def body(r, peeled):
                for q in range(SPAN):
                    n = r * SPAN + q
                    act.wait_ge(v_in[q // 2], r * 16 + 16)
                    if not (peeled and q < 4):
                        act.wait_ge(used, n - 3)
                    nc.scalar.activation(vh[:, q % 4], raw[:, q // 2, q % 2], ACT.Copy).then_inc(v_high, 1)
                    act.wait_ge(a_there, n + 1)
                    nc.scalar.activation(ah[:, q % 4], a[:, q % 4], ACT.Copy).then_inc(a_high, 1)
            body(0, True)
            with act.Fori(1, SETS) as r:
                body(r, False)

        @block.vector
        def _(dve):
            def low(n, q):
                dve.wait_ge(a_high, n + 1)
                nc.vector.tensor_tensor(al[:, q % 4], a[:, q % 4], ah[:, q % 4].bitcast(F32), ALU.subtract).then_inc(a_low, 1)

            def body(r, peeled):
                for q in range(SPAN):
                    n = r * SPAN + q
                    dve.wait_ge(h_in[q // 2], r * 16 + 16)
                    dve.wait_ge(g_in[q // QUAD], r * 16 + 16)
                    if not (peeled and q < 4):
                        dve.wait_ge(a_low, n - 3)
                    nc.vector.tensor_tensor(a[:, q % 4].rearrange("p (b t) -> p b t", t=TB),
                                            hin[:, q // 2, q % 2].rearrange("p (b t) -> p b t", t=TB),
                                            gin[:, q // QUAD, :, q % QUAD], ALU.mult).then_inc(a_there, 1)
                    if not (peeled and q < 1):
                        if not (peeled and q < 5):
                            dve.wait_ge(used, n - 4)
                        low(n - 1, (q - 1) % SPAN)
            body(0, True)
            with dve.Fori(1, SETS) as r:
                body(r, False)
            low(NCH - 1, SPAN - 1)
            dve.wait_ge(used, NCH)
            for t in range(NT):
                nc.vector.tensor_tensor(resid[:, t].rearrange("p (a c) -> p a c", a=2), ps[:, t],
                                        resid[:, t].rearrange("p (a c) -> p a c", a=2), ALU.add)

        @block.tensor
        def _(pe):
            def body(r, first, last_set):
                for q in range(SPAN):
                    n = r * SPAN + q
                    pe.wait_ge(v_low, n + 1)
                    pe.wait_ge(a_low, n + 1)
                    for t in range(NT):
                        ts = slice(t * P, (t + 1) * P)
                        for c in range(2):
                            cs = slice(c * T, (c + 1) * T)
                            last = three_pass(nc, ps[:, t, c], ah[:, q % 4, ts], al[:, q % 4, ts], vh[:, q % 4, cs],
                                              vl[:, q % 4, cs], first and q == 0, last_set and q == SPAN - 1)
                    last.then_inc(used, 1)
            body(0, True, False)
            with pe.Fori(1, SETS - 1) as r:
                body(r, False, False)
            body(SETS - 1, False, True)


def gla_stage(nc, name, consts, qkT, gv, gg, glrT, w_alpha, b_alpha, gain, mixed):
    scan_mask, causal, ident = consts["scan_mask"], consts["causal"], consts["ident"]
    M = GPAIRS
    with Scope(nc, name) as s:
        ze = s.sb("z_e", [P, 2, M, T])
        z, e = ze[:, 0], ze[:, 1]
        lt = s.sb("ln_end", [P, 2, M, T])
        ln, to_end = lt[:, 0], lt[:, 1]
        b = s.sb("b", [P, M, T])
        eb = s.sb("exp_b", [P, M, T])
        enb = s.sb("exp_nb", [P, M, T])
        eke = s.sb("exp_end", [P, M, T])
        qd = s.sb("q_dec", [P, M, T])
        ki = s.sb("k_inv", [P, M, T])
        ke = s.sb("k_end", [P, M, T])
        keN = s.sb("k_end_rows", [P, NT, M, P])
        att = s.sb("att", [P, NT, GH, P])
        state = s.sb("state", [P, M, NCHUNK, GDV])
        o = s.sb("o", [P, NT, GH, GDV])
        sq = ze[:].rearrange("p a m t -> p (a m) t")
        ss = s.sb("ss", [P, NT * GH])
        root = s.sb("root", [P, NT * GH])
        sg = lt[:].rearrange("p a m t -> p (a m) t")
        tok = consts["tok"]
        zp = s.ps("psA", [P, 2, T])
        kt = s.ps("psT", [P, 2, T])
        kv = s.ps("psKV", [P, M, 2, NCHUNK // 2, GDV])
        z_done, zb, absd, ed, lnd, scand, expd, ended, eke_d = (s.sem(x) for x in (
            "z_done", "z_there", "abs", "exp", "ln", "scanned", "exps", "end_diff", "exp_end"))
        chain, ke_there, turned, rows, kv_done = (s.sem(x) for x in ("chain", "k_end", "turned", "rows", "kv_done"))
        dec_there, states, a_done, masked, o_done, o_taken, silu, ssd, rooted = (s.sem(x) for x in (
            "dec", "states", "a_done", "masked", "o_done", "o_taken", "silu", "ss", "rooted"))
        block = s.block()

        @block.tensor
        def _(pe):
            for m in range(M):
                last = nc.tensor.matmul(zp[:, m], w_alpha[:, m * P:(m + 1) * P], glrT[0:GRANK, :], start=True, stop=True)
            last.then_inc(z_done, 1)
            pe.wait_ge(ke_there, 1)
            for m in range(M):
                for t in range(NT):
                    last = nc.tensor.transpose(kt[:, m, t * P:(t + 1) * P], ke[:, m, t * P:(t + 1) * P], ident[:])
                last.then_inc(turned, 1)
            def scores(t):
                if t:
                    pe.wait_ge(masked, t)
                for h in range(GH):
                    m, r = h // 2, slice(GDK * (h % 2), GDK * (h % 2) + GDK)
                    last = nc.tensor.matmul(zp[:, h % 2, m * P:(m + 1) * P], ki[r, m, t * P:(t + 1) * P],
                                            qd[r, m, t * P:(t + 1) * P], start=True, stop=True)
                last.then_inc(a_done, 1)
            pe.wait_ge(dec_there, 1)
            scores(0)
            pe.wait_ge(rows, 1)
            for c in range(NCHUNK - 1):
                r, t = slice(GCHUNK * (c % 2), GCHUNK * (c % 2) + GCHUNK), c // 2
                for h in range(GH):
                    m, hh = h // 2, h % 2
                    last = nc.tensor.matmul(kv[GDK * hh:GDK * hh + GDK, m, c % 2, c // 2], keN[r, t, m, GDK * hh:GDK * hh + GDK],
                                            gv[r, t, h * GDV:(h + 1) * GDV], start=True, stop=True)
            last.then_inc(kv_done, 1)
            pe.wait_ge(states, 1)
            for t in range(NT):
                pe.wait_ge(masked, t + 1)
                if t:
                    pe.wait_ge(o_taken, t)
                for h in range(GH):
                    m, hh = h // 2, h % 2
                    r, cols = slice(GDK * hh, GDK * hh + GDK), slice(m * GDV, (m + 1) * GDV)
                    last = nc.tensor.matmul(kt[:, hh, cols], att[:, t, h], gv[:, t, h * GDV:(h + 1) * GDV],
                                            start=True, stop=False)
                    for c in (2 * t, 2 * t + 1):
                        half = GCHUNK * (c % 2)
                        last = nc.tensor.matmul(kt[half:half + GCHUNK, hh, cols], qd[r, m, c * GCHUNK:(c + 1) * GCHUNK],
                                                state[r, m, c], start=False, stop=True)
                last.then_inc(o_done, 1)
                if t + 1 < NT:
                    scores(t + 1)

        @block.scalar
        def _(act):
            act.wait_ge(zb, 1)
            nc.scalar.activation(e, z, ACT.Abs).then_inc(absd, 1)
            act.wait_ge(absd, 1)
            nc.scalar.activation(ln, e, ACT.Exp, scale=-1.0).then_inc(ed, 1)
            act.wait_ge(ed, 1)
            nc.scalar.activation(e, ln, ACT.Ln, bias=1.0).then_inc(lnd, 1)
            act.wait_ge(scand, M)
            nc.scalar.activation(eb[:], b[:], ACT.Exp, scale=1.0 / GATE_TAU).then_inc(expd, 1)
            nc.scalar.activation(enb[:], b[:], ACT.Exp, scale=-1.0 / GATE_TAU).then_inc(expd, 1)
            act.wait_ge(ended, 1)
            nc.scalar.activation(eke[:], to_end, ACT.Exp, scale=1.0 / GATE_TAU).then_inc(eke_d, 1)
            act.wait_ge(turned, M)
            nc.scalar.activation(keN[:].rearrange("p t m k -> p m t k"), kt[:].rearrange("p m (t k) -> p m t k", k=P),
                                 ACT.Copy).then_inc(rows, 1)
            nc.scalar.activation(sg, gg[:], ACT.Sigmoid).then_inc(silu, 1)
            for t in range(NT):
                act.wait_ge(o_done, t + 1)
                nc.scalar.activation(o[:, t].rearrange("p (m a) v -> p a m v", a=2),
                                     kt[:, :, 0:M * GDV].rearrange("p a (m v) -> p a m v", v=GDV), ACT.Copy).then_inc(o_taken, 1)
            act.wait_ge(ssd, 1)
            nc.scalar.activation(root[:], ss[:], ACT.Sqrt).then_inc(rooted, 1)

        @block.vector
        def _(dve):
            ch = Chain(dve, chain)
            link = ch.link
            nc.vector.memset(att[:], 0.0)
            nc.vector.memset(state[:, :, 0], 0.0)
            dve.wait_ge(z_done, 1)
            for m in range(M):
                last = nc.vector.tensor_scalar(z[:, m], zp[:, m], b_alpha[:, m:m + 1], None, ALU.add)
            last.then_inc(zb, 1)
            dve.wait_ge(lnd, 1)
            link(nc.vector.scalar_tensor_tensor(ln, z, 0.0, e, ALU.min, ALU.subtract))
            for m in range(M):
                nc.vector.tensor_tensor_scan(b[:, m], scan_mask[:], ln[:, m], 0.0, ALU.mult, ALU.add).then_inc(scand, 1)
            dve.wait_ge(scand, M)
            bc = b[:].rearrange("p m (n c) -> p (m n) c", c=GCHUNK)
            end = bc[:, :, GCHUNK - 1:GCHUNK].to_broadcast([P, M * NCHUNK, GCHUNK])
            nc.vector.tensor_tensor(to_end.rearrange("p m (n c) -> p (m n) c", c=GCHUNK), end, bc, ALU.subtract).then_inc(ended, 1)
            dve.wait_ge(expd, 2)
            nc.vector.scalar_tensor_tensor(qd[:], qkT[:, 0:M], float(GDK) ** -0.5, eb[:], ALU.mult, ALU.mult)
            nc.vector.tensor_tensor(ki[:], qkT[:, M:2 * M], enb[:], ALU.mult).then_inc(dec_there, 1)
            dve.wait_ge(eke_d, 1)
            nc.vector.tensor_tensor(ke[:], qkT[:, M:2 * M], eke[:], ALU.mult).then_inc(ke_there, 1)

            def mask(t):
                dve.wait_ge(a_done, t + 1)
                nc.vector.copy_predicated(att[:, t].rearrange("p (m a) i -> p a m i", a=2), causal[:].rearrange("p (a m i) -> p a m i", a=2, m=M),
                                          zp[:, :, 0:M * P].rearrange("p a (m i) -> p a m i", i=P)).then_inc(masked, 1)
            mask(0)
            dve.wait_ge(kv_done, 1)
            for c in range(NCHUNK - 1):
                for m in range(M):
                    new = kv[:, m, c % 2, c // 2]
                    if c == 0:
                        last = nc.vector.tensor_copy(state[:, m, 1], new)
                    else:
                        at = (c + 1) * GCHUNK - 1
                        last = nc.vector.scalar_tensor_tensor(state[:, m, c + 1], state[:, m, c], eb[:, m, at:at + 1], new,
                                                              ALU.mult, ALU.add)
                link(last)
            nc.vector.tensor_copy(tok[:], eb[:, 0, 0:1]).then_inc(states, 1)
            for t in range(1, NT):
                mask(t)
            dve.wait_ge(silu, 1)
            link(nc.vector.tensor_tensor(sg, sg, gg[:], ALU.mult))
            link(nc.vector.tensor_tensor(sg, sg, gain[:].unsqueeze(1).to_broadcast([P, NT, GV_W]), ALU.mult))
            for t in range(NT):
                dve.wait_ge(o_taken, t + 1)
                ot = o[:, t].rearrange("p h v -> p (h v)")
                link(nc.vector.tensor_tensor(sq[:, t], ot, ot, ALU.mult))
                link(nc.vector.tensor_reduce(ss[:, t * GH:(t + 1) * GH], sq[:, t].rearrange("p (h v) -> p h v", v=GDV), AX.X, ALU.add))
            nc.vector.tensor_scalar(ss[:], ss[:], 1.0 / GDV, EPS, ALU.mult, ALU.add).then_inc(ssd, 1)
            dve.wait_ge(rooted, 1)
            link(nc.vector.reciprocal(root[:], root[:]))
            r = root[:].unsqueeze(2).to_broadcast([P, NT * GH, GDV])
            of = o[:].rearrange("p t h v -> p (t h) v")
            link(nc.vector.tensor_tensor(of, of, r, ALU.mult))
            nc.vector.tensor_tensor(mixed[:, :, 0:GV_W], o[:].rearrange("p t h v -> p t (h v)"), sg, ALU.mult)


def attention_stage(nc, name, consts, bias, qkT, av, mixed):
    ident = consts["ident"]
    scale = float(AHD) ** -0.5
    A2 = AH * AHD // P
    units = [(t, h) for t in range(NT) for h in range(AH)]
    with Scope(nc, name) as s:
        sc = s.sb("scores", [P, 2, T])
        mx = s.sb("mx", [P, NT * AH])
        nb = s.sb("nb", [P, NT * AH])
        pr = s.sb("probs", [P, 2, T])
        den = s.sb("den", [P, NT * AH])
        rden = s.sb("rden", [P, NT * AH])
        pT = s.sb("probsT", [P, 2, T])
        ps_s = s.ps("ps_s", [P, 2, T])
        ps_t = s.ps("ps_t", [P, 2, T])
        ps_o = s.ps("ps_o", [P, 2, T])
        qk_done, biased, neg, prob, turned, kept, o_done, recip, o_taken = (s.sem(x) for x in (
            "qk_done", "biased", "neg", "prob", "turned", "kept", "o_done", "recip", "o_taken"))
        block = s.block()

        @block.tensor
        def _(pe):
            def qk(u):
                t, h = units[u]
                r = slice(AHD * (h % 2), AHD * (h % 2) + AHD)
                wait(pe, biased, u - 1)
                nc.tensor.matmul(ps_s[:, u % 2, 0:(t + 1) * P], qkT[r, h // 2, t * P:(t + 1) * P],
                                 qkT[r, A2 + h // 2, 0:(t + 1) * P], start=True, stop=True).then_inc(qk_done, 1)

            def turn(u):
                t, h = units[u]
                pe.wait_ge(prob, u + 1)
                wait(pe, kept, u - 1)
                for k in range(t + 1):
                    last = nc.tensor.transpose(ps_t[:, u % 2, k * P:(k + 1) * P], pr[:, u % 2, k * P:(k + 1) * P], ident[:])
                last.then_inc(turned, 1)

            def pv(u):
                t, h = units[u]
                pe.wait_ge(kept, u + 1)
                wait(pe, o_taken, u - 1)
                for k in range(t + 1):
                    last = nc.tensor.matmul(ps_o[:, u % 2, 0:AHD], pT[:, u % 2, k * P:(k + 1) * P],
                                            av[:, k, h * AHD:(h + 1) * AHD], start=(k == 0), stop=(k == t))
                last.then_inc(o_done, 1)

            n = len(units)
            for u in range(n + 2):
                if u < n:
                    qk(u)
                if 1 <= u <= n:
                    turn(u - 1)
                if u >= 2:
                    pv(u - 2)

        @block.scalar
        def _(act):
            for u, (t, h) in enumerate(units):
                w = (t + 1) * P
                act.wait_ge(neg, u + 1)
                wait(act, turned, u - 1)
                nc.scalar.activation(pr[:, u % 2, 0:w], sc[:, u % 2, 0:w], ACT.Exp, bias=nb[:, u:u + 1], scale=scale,
                                     accum_out=den[:, u:u + 1]).then_inc(prob, 1)
                act.wait_ge(turned, u + 1)
                wait(act, o_done, u - 1)
                nc.scalar.activation(pT[:, u % 2, 0:w], ps_t[:, u % 2, 0:w], ACT.Copy).then_inc(kept, 1)

        @block.vector
        def _(dve):
            def finish(u):
                t, h = units[u]
                dve.wait_ge(prob, u + 1)
                nc.vector.reciprocal(rden[:, u:u + 1], den[:, u:u + 1]).then_inc(recip, 1)
                dve.wait_ge(recip, u + 1)
                dve.wait_ge(o_done, u + 1)
                nc.vector.tensor_scalar(mixed[:, t, GV_W + h * AHD:GV_W + (h + 1) * AHD], ps_o[:, u % 2, 0:AHD],
                                        rden[:, u:u + 1], None, ALU.mult).then_inc(o_taken, 1)

            for u, (t, h) in enumerate(units):
                w = (t + 1) * P
                dve.wait_ge(qk_done, u + 1)
                wait(dve, prob, u - 1)
                nc.vector.tensor_tensor_reduce(out=sc[:, u % 2, 0:w], in0=ps_s[:, u % 2, 0:w], in1=bias[:, h, T - w:T],
                                               scale=1.0, scalar=NEG, op0=ALU.add, op1=ALU.max,
                                               accum_out=mx[:, u:u + 1]).then_inc(biased, 1)
                dve.wait_ge(biased, u + 1)
                nc.vector.tensor_scalar(nb[:, u:u + 1], mx[:, u:u + 1], -scale, None, ALU.mult).then_inc(neg, 1)
                if u >= 3:
                    finish(u - 3)
            for u in range(len(units) - 3, len(units)):
                finish(u)


def split_rows_stage(nc, name, rows, ident, xh, xl):
    with Scope(nc, name) as s:
        ps = s.ps("ps", [P, KD, T])
        turned, hi = s.sem("turned"), s.sem("hi")
        block = s.block()

        @block.tensor
        def _(pe):
            for c in range(KD):
                for t in range(NT):
                    last = nc.tensor.transpose(ps[:, c, t * P:(t + 1) * P], rows[:, t, c * P:(c + 1) * P], ident[:])
                last.then_inc(turned, 1)

        @block.scalar
        def _(act):
            for c in range(KD):
                act.wait_ge(turned, c + 1)
                nc.scalar.activation(xh[:, c], ps[:, c], ACT.Copy).then_inc(hi, 1)

        @block.vector
        def _(dve):
            for c in range(KD):
                dve.wait_ge(hi, c + 1)
                nc.vector.tensor_tensor(xl[:, c], ps[:, c], xh[:, c].bitcast(F32), ALU.subtract)


def recurrent_stage(nc, name, A, gxT, xh, xl):
    G = RT
    with Scope(nc, name) as s:
        wr = s.sb("w_rgate", [P, G, P])
        wi = s.sb("w_igate", [P, G, P])
        cw = s.sb("conv_w", [P, G, CONV])
        vec = s.sb("vec", [P, 4, G])
        sp8 = s.sb("sp8", [P, 8, G])
        xc = s.sb("xc", [P, G, T])
        rg = s.sb("r", [P, G, T])
        ig = s.sb("i", [P, G, T])
        a = s.sb("a", [P, G, T])
        ps = s.ps("ps", [P, 3, 2, T])
        loaded, chain, conved, gated, g_done, exps, lam = (s.sem(x) for x in (
            "loaded", "chain", "conved", "gated", "g_done", "exps", "lam"))
        lam_abs, lam_exp, sp_there, rooted, q_there, u_there, gelus, y_there, hi = (s.sem(x) for x in (
            "lam_abs", "lam_exp", "sp_there", "rooted", "q_there", "u_there", "gelus", "y_there", "hi"))
        block = s.block()

        @block.sync
        def _(sp):
            for dst, src in ((wr[:], A["w_rgate"]), (wi[:], A["w_igate"]), (cw[:], A["conv_w"]), (vec[:, 0], A["conv_b"]),
                             (vec[:, 1], A["b_rgate"]), (vec[:, 2], A["b_igate"]), (vec[:, 3], A["lam"])):
                sp.dma_start(dst, src).then_inc(loaded, 16)

        LOADED = 7 * 16

        @block.vector
        def _(dve):
            ch = Chain(dve, chain)
            link = ch.link
            dve.wait_ge(loaded, LOADED)
            for g in range(G):
                x = gxT[:, G + g]
                link(nc.vector.tensor_scalar(xc[:, g], x, cw[:, g, 3:4], vec[:, 0, g:g + 1], ALU.mult, ALU.add))
                for k in (1, 2, 3):
                    ins = nc.vector.scalar_tensor_tensor(xc[:, g, k:], x[:, 0:T - k], cw[:, g, 3 - k:4 - k], xc[:, g, k:],
                                                         ALU.mult, ALU.add)
                    if k < 3:
                        link(ins)
                    else:
                        ins.then_inc(conved, 1)
            dve.wait_ge(lam_exp, 1)
            e, z, z2, acc, tmp = (sp8[:, k] for k in range(1, 6))
            link(nc.vector.tensor_scalar(tmp, e, 2.0, None, ALU.add))
            link(nc.vector.reciprocal(tmp, tmp))
            link(nc.vector.tensor_tensor(z, e, tmp, ALU.mult))
            link(nc.vector.tensor_tensor(z2, z, z, ALU.mult))
            link(nc.vector.tensor_scalar(acc, z2, 1.0 / 17, 1.0 / 15, ALU.mult, ALU.add))
            for k in (13, 11, 9, 7, 5, 3, 1):
                link(nc.vector.tensor_tensor(acc, acc, z2, ALU.mult))
                link(nc.vector.tensor_scalar(acc, acc, 1.0 / k, None, ALU.add))
            link(nc.vector.tensor_tensor(acc, acc, z, ALU.mult))
            link(nc.vector.tensor_scalar(acc, acc, 2.0, None, ALU.mult))
            link(nc.vector.tensor_scalar(tmp, vec[:, 3], -1.0, 0.0, ALU.mult, ALU.max))
            link(nc.vector.tensor_tensor(acc, acc, tmp, ALU.add))
            link(nc.vector.tensor_scalar(sp8[:, 6], acc, -LRU_C, None, ALU.mult))
            nc.vector.tensor_scalar(sp8[:, 7], acc, LRU_C, None, ALU.mult).then_inc(sp_there, 1)
            for g in range(G):
                x = gxT[:, G + g]
                dve.wait_ge(exps, 2 * (g + 1))
                link(nc.vector.tensor_tensor(x, a[:, g], a[:, g], ALU.mult))
                nc.vector.scalar_tensor_tensor(x, x, 1.0, rg[:, g], ALU.add, ALU.mult).then_inc(q_there, 1)
                link(nc.vector.tensor_tensor(xc[:, g], xc[:, g], ig[:, g], ALU.mult))
            for g in range(G):
                dve.wait_ge(rooted, g + 1)
                link(nc.vector.tensor_tensor(xc[:, g], xc[:, g], rg[:, g], ALU.mult))
                link(nc.vector.tensor_tensor_scan(ig[:, g], a[:, g], xc[:, g], 0.0, ALU.mult, ALU.add))
                dve.wait_ge(gelus, g + 1)
                nc.vector.tensor_tensor(xc[:, g], gxT[:, g], ig[:, g], ALU.mult).then_inc(y_there, 1)
                if g:
                    dve.wait_ge(hi, g)
                    nc.vector.tensor_tensor(xl[:, g - 1], xc[:, g - 1], xh[:, g - 1].bitcast(F32), ALU.subtract)
            dve.wait_ge(hi, G)
            nc.vector.tensor_tensor(xl[:, G - 1], xc[:, G - 1], xh[:, G - 1].bitcast(F32), ALU.subtract)

        @block.scalar
        def _(act):
            act.wait_ge(loaded, LOADED)
            nc.scalar.activation(sp8[:, 0], vec[:, 3], ACT.Abs).then_inc(lam_abs, 1)
            act.wait_ge(lam_abs, 1)
            nc.scalar.activation(sp8[:, 1], sp8[:, 0], ACT.Exp, scale=-1.0).then_inc(lam_exp, 1)
            for g in range(G):
                act.wait_ge(g_done, g + 1)
                nc.scalar.activation(rg[:, g], ps[:, g % 3, 0], ACT.Sigmoid, bias=vec[:, 1, g:g + 1])
                nc.scalar.activation(ig[:, g], ps[:, g % 3, 1], ACT.Sigmoid, bias=vec[:, 2, g:g + 1]).then_inc(gated, 1)
            act.wait_ge(sp_there, 1)
            act.wait_ge(gated, G)
            for g in range(G):
                nc.scalar.activation(a[:, g], rg[:, g], ACT.Exp, scale=sp8[:, 6, g:g + 1]).then_inc(exps, 1)
                nc.scalar.activation(rg[:, g], rg[:, g], ACT.Tanh, scale=sp8[:, 7, g:g + 1]).then_inc(exps, 1)
            for g in range(G):
                act.wait_ge(q_there, g + 1)
                nc.scalar.activation(rg[:, g], gxT[:, G + g], ACT.Sqrt).then_inc(rooted, 1)
            for g in range(G):
                nc.scalar.activation(gxT[:, g], gxT[:, g], ACT.Gelu_apprx_tanh).then_inc(gelus, 1)
            for g in range(G):
                act.wait_ge(y_there, g + 1)
                nc.scalar.activation(xh[:, g], xc[:, g], ACT.Copy).then_inc(hi, 1)

        @block.tensor
        def _(pe):
            for g in range(G):
                pe.wait_ge(conved, g + 1)
                wait(pe, gated, g - 2)
                nc.tensor.matmul(ps[:, g % 3, 0], wr[:, g], xc[:, g], start=True, stop=True)
                nc.tensor.matmul(ps[:, g % 3, 1], wi[:, g], xc[:, g], start=True, stop=True).then_inc(g_done, 1)


def final_stage(nc, name, resid, final_norm, out):
    with Scope(nc, name) as s:
        xn = s.sb("xn", [P, NT, D])
        gain = s.sb("gain", [P, D])
        ss = s.sb("ss", [P, NT])
        rs = s.sb("rs", [P, NT])
        gain_in, squared, mean, rooted, chain, there, stored = (s.sem(x) for x in (
            "gain_in", "squared", "mean", "rooted", "chain", "there", "stored"))
        block = s.block()

        @block.sync
        def _(sp):
            sp.dma_start(gain[:], final_norm.partition_broadcast(P)).then_inc(gain_in, 16)
            rows = out.rearrange("(t p) d -> p t d", p=P)
            for t in range(NT):
                sp.wait_ge(there, t + 1)
                sp.dma_start(rows[:, t], xn[:, t]).then_inc(stored, 16)
            sp.wait_ge(stored, NT * 16)

        @block.scalar
        def _(act):
            for t in range(NT):
                nc.scalar.activation(xn[:, t], resid[:, t], ACT.Square, accum_out=ss[:, t:t + 1]).then_inc(squared, 1)
            act.wait_ge(mean, 1)
            nc.scalar.activation(rs[:], ss[:], ACT.Sqrt).then_inc(rooted, 1)

        @block.vector
        def _(dve):
            ch = Chain(dve, chain)
            dve.wait_ge(squared, NT)
            nc.vector.tensor_scalar(ss[:], ss[:], 1.0 / D, EPS, ALU.mult, ALU.add).then_inc(mean, 1)
            dve.wait_ge(rooted, 1)
            ch.link(nc.vector.reciprocal(rs[:], rs[:]))
            dve.wait_ge(gain_in, 16)
            for t in range(NT):
                ch.link(nc.vector.tensor_scalar(xn[:, t], resid[:, t], rs[:, t:t + 1], None, ALU.mult))
                nc.vector.tensor_tensor(xn[:, t], xn[:, t], gain[:], ALU.mult).then_inc(there, 1)


def trunk(nc, A, out):
    Scope.HELD.clear()
    hT = nc.dram_tensor("hidden_scratch", (NCH // 2, P, 2 * T), F32).ap()
    gT = nc.dram_tensor("gate_scratch", (T // TB, P, NKEYS * TB), F32).ap()
    with Scope(nc, "main") as s:
        resid = s.sb("resid", [P, NT, D])
        gains = s.sb("gains", [P, 4, KD])
        ident = s.sb("ident", [P, P])
        iota = s.sb("iota", [P, P])
        cand_iota = s.sb("cand_iota", [P, NCAND])
        tok = s.sb("tok", [P, 1])
        xh = s.sb("x_hi", [P, KD, T], F32R)
        xl = s.sb("x_lo", [P, KD, T], F32R)
        consts = {"ident": ident, "iota": iota, "cand_iota": cand_iota, "tok": tok}
        with Scope(nc, "load") as l:
            loaded = l.sem("loaded")
            block = l.block()

            @block.sync
            def _(sp):
                loads = ((resid[:], A["x"].rearrange("(t p) d -> p t d", p=P)), (gains[:], A["gains"]), (ident[:], A["ident"]),
                         (iota[:], A["iota"].partition_broadcast(P)), (cand_iota[:], A["iota"][0:NCAND].partition_broadcast(P)))
                for dst, src in loads:
                    sp.dma_start(dst, src).then_inc(loaded, 16)
                sp.wait_ge(loaded, len(loads) * 16)

        norm_stage(nc, "mix0", resid, gains[:, 0], ident, xh, xl)
        with Scope(nc, "l0") as m:
            byc = m.sb("by_column", [P, 12, T])
            byr = m.sb("by_row", [P, NT, 3 * T])
            glrT = m.sb("gate_rankT", [P, T])
            low_rank_stage(nc, "glr", A["w_glr"], xh, xl, glrT)
            project_stage(nc, "abT", A["w_ab_T"], 6, xh, xl, byc, True)
            project_stage(nc, "abN", A["w_ab_N"], 6, xh, xl, byr, False)
            mixed = m.sb("mixed", [P, NT, D])
            with Scope(nc, "gla_c") as g:
                scan_mask, causal = g.sb("scan_mask", [P, T]), g.sb("causal", [P, T], I32)
                w_alpha, b_alpha, gain = g.sb("w_alpha", [GRANK, GH * GDK]), g.sb("b_alpha", [P, GPAIRS]), g.sb("gain", [P, GV_W])
                consts |= {"scan_mask": scan_mask, "causal": causal}
                with Scope(nc, "gla_l") as l:
                    loaded = l.sem("loaded")
                    block = l.block()

                    @block.sync
                    def _(sp):
                        loads = ((scan_mask[:], A["scan_mask"].partition_broadcast(P)), (causal[:], A["causal"]), (w_alpha[:], A["w_alpha"]),
                                 (b_alpha[:], A["b_alpha"]), (gain[:], A["head_gain"].partition_broadcast(P)))
                        for dst, src in loads:
                            sp.dma_start(dst, src).then_inc(loaded, 16)
                        sp.wait_ge(loaded, len(loads) * 16)
                gla_stage(nc, "gla", consts, byc[:, 0:4], byr[:, :, 0:T], byr[:, :, T:2 * T], glrT, w_alpha, b_alpha, gain, mixed)
            with Scope(nc, "att_c") as g:
                bias = g.sb("bias", [P, AH, T])
                with Scope(nc, "att_l") as l:
                    loaded = l.sem("loaded")
                    block = l.block()

                    @block.sync
                    def _(sp):
                        sp.dma_start(bias[:], A["att_bias"]).then_inc(loaded, 16)
                        sp.wait_ge(loaded, 16)
                attention_stage(nc, "att", consts, bias, byc[:, 4:12], byr[:, :, 2 * T:3 * T], mixed)
            split_rows_stage(nc, "mixedT", mixed, ident, xh, xl)
        project_stage(nc, "out0", A["w_out0"], D // BC, xh, xl, resid, False, add=True)
        expert_stages(nc, "peer0", A, 0, resid, gains[:, 2], consts, hT, gT, xh, xl)

        Scope.reset(nc)
        norm_stage(nc, "mix1", resid, gains[:, 1], ident, xh, xl)
        with Scope(nc, "l1") as m:
            gxT = m.sb("gate_x", [P, 2 * RT, T])
            project_stage(nc, "c_in", A["w_c_in"], 2 * D // BC, xh, xl, gxT, True)
            recurrent_stage(nc, "rec", A, gxT, xh, xl)
        project_stage(nc, "out1", A["w_c_out"], D // BC, xh, xl, resid, False, add=True)
        expert_stages(nc, "peer1", A, 1, resid, gains[:, 3], consts, hT, gT, xh, xl)
        final_stage(nc, "final", resid, A["final_norm"], out)


def low_rank_stage(nc, name, dram, xh, xl, dest):
    with Scope(nc, name) as s:
        raw, wh, wl = s.sb("raw", [P, KD, P]), s.sb("hi", [P, KD, P], F32R), s.sb("lo", [P, KD, P], F32R)
        ps = s.ps("ps", [P, T])
        loaded, high, low, done = s.sem("loaded"), s.sem("high"), s.sem("low"), s.sem("done")
        block = s.block()

        @block.sync
        def _(sp):
            sp.dma_start(raw[:].rearrange("p k c -> p (k c)"), dram).then_inc(loaded, 16)

        @block.scalar
        def _(act):
            act.wait_ge(loaded, 16)
            nc.scalar.activation(wh[:], raw[:], ACT.Copy).then_inc(high, 1)

        @block.vector
        def _(dve):
            dve.wait_ge(high, 1)
            nc.vector.tensor_tensor(wl[:], raw[:], wh[:].bitcast(F32), ALU.subtract).then_inc(low, 1)
            dve.wait_ge(done, 1)
            nc.vector.tensor_copy(dest[:], ps[:])

        @block.tensor
        def _(pe):
            pe.wait_ge(low, 1)
            for d in range(KD):
                last = three_pass(nc, ps[:], wh[:, d], wl[:, d], xh[:, d], xl[:, d], d == 0, d == KD - 1)
            last.then_inc(done, 1)


def expert_stages(nc, name, A, layer, resid, gain, consts, hT, gT, xh, xl):
    norm_stage(nc, f"{name}n", resid, gain, consts["ident"], xh, xl)
    with Scope(nc, f"{name}s") as s:
        scores = s.sb("scores", [P, NT, 2 * PH, NKEYS])
        query_stage(nc, f"{name}q", A["w_query"][layer], A["keysT"][layer], xh, xl, scores)
        up_stage(nc, f"{name}u", A["uT"][layer], hT, gT, consts, xh, xl, scores)
    down_stage(nc, f"{name}v", A["v"][layer], hT, gT, resid)


def kernel(**inputs):
    import concourse.bacc as bacc
    from concourse.bass_utils import run_bass_kernel_spmd

    x = {k: np.asarray(v) for k, v in inputs.items()}

    def blocks(w, starts, width=BC):
        return np.ascontiguousarray(np.stack([w[:, c:c + width].reshape(KD, P, width).transpose(1, 0, 2).reshape(P, KD * width)
                                              for c in starts]))

    def columns(v):
        return np.ascontiguousarray(v.reshape(-1, P).T)

    qk, vw, aw = GH * GDK, GV_W, AH * AHD
    at_gv, at_gg, at_glr = 2 * qk, 2 * qk + vw, 2 * qk + 2 * vw
    at_aq = at_glr + GRANK
    at_ak, at_av = at_aq + aw, at_aq + 2 * aw
    w_in = x["ab_w_in"][0]
    wide = range(0, D, BC)

    delta = (T - P) + np.arange(P)[:, None] - np.arange(T)[None, :]
    count = np.zeros(delta.shape)
    for window, dil in BRANCHES:
        count += (delta >= 0) & (delta % dil == 0) & (delta <= window)
    slopes = 2.0 ** (-8.0 * np.arange(1, AH + 1) / AH)
    with np.errstate(divide="ignore"):
        penalty = np.where(count > 0, np.log(np.maximum(count, 1)), -1e30)
    att_bias = (math.sqrt(AHD) * (penalty[:, None, :] - slopes[None, :, None] * delta[:, None, :])).astype(np.float32)
    j, i = np.arange(P)[:, None], np.arange(P)[None, :]
    causal = np.tile(((j <= i) & (j // GCHUNK == i // GCHUNK)).astype(np.int32), (1, GH))

    arrays = {
        "x": x["x"].reshape(T, D),
        "gains": np.stack([columns(x[n][k]) for n in ("mix_norm", "ffn_norm") for k in range(2)], axis=1),
        "ident": np.eye(P, dtype=np.float32),
        "iota": np.arange(P, dtype=np.float32),
        "scan_mask": (np.arange(T) % GCHUNK != 0).astype(np.float32),
        "causal": causal,
        "att_bias": att_bias,
        "w_glr": blocks(w_in, [at_glr], P)[0],
        "w_ab_T": blocks(w_in, [0, qk, at_aq, at_aq + BC, at_ak, at_ak + BC]),
        "w_ab_N": blocks(w_in, [at_gv, at_gv + BC, at_gg, at_gg + BC, at_av, at_av + BC]),
        "w_alpha": x["gla_w_alpha"][0],
        "b_alpha": columns(x["gla_b_alpha"][0]),
        "head_gain": x["gla_head_gain"][0],
        "w_out0": blocks(x["ab_w_out"][0], wide),
        "w_c_in": blocks(x["c_w_in"][0], range(0, 2 * D, BC)),
        "conv_w": x["c_conv_w"][0].reshape(CONV, RT, P).transpose(2, 1, 0),
        "conv_b": columns(x["c_conv_b"][0]),
        "w_rgate": x["c_w_rgate"][0].transpose(1, 0, 2),
        "w_igate": x["c_w_igate"][0].transpose(1, 0, 2),
        "b_rgate": columns(x["c_b_rgate"][0]),
        "b_igate": columns(x["c_b_igate"][0]),
        "lam": columns(x["c_lambda"][0]),
        "w_c_out": blocks(x["c_w_out"][0], wide),
        "w_query": np.stack([blocks(x["peer_w_query"][k], range(0, 2 * PH * P, BC)) for k in range(2)]),
        "keysT": x["peer_sub_keys"].transpose(0, 4, 1, 2, 3).reshape(2, P, 2 * PH * NKEYS),
        "uT": x["peer_u"].reshape(2, NCH // 2, 2, P, KD, P).transpose(0, 1, 5, 2, 4, 3).reshape(2, NCH // 2, P, 2 * KD * P),
        "v": x["peer_v"],
        "final_norm": x["final_norm"],
    }
    nc = bacc.Bacc("TRN2", target_bir_lowering=False, num_devices=1)
    feed, A = {}, {}
    for name, a in arrays.items():
        feed[f"in_{name}"] = np.ascontiguousarray(a)
        A[name] = nc.dram_tensor(f"in_{name}", a.shape, mybir.dt.from_np(a.dtype), kind="ExternalInput").ap()
    out = nc.dram_tensor("out_0", (T, D), F32, kind="ExternalOutput").ap()
    trunk(nc, A, out)
    r = run_bass_kernel_spmd(nc, [feed], core_ids=[0])
    return r.results[0]["out_0"].reshape(inputs["x"].shape)
```

```python
import math
from contextlib import ExitStack

import numpy as np

import concourse.bass as bass
from concourse import mybir

F32 = mybir.dt.float32
F32R = mybir.dt.float32r
I32 = mybir.dt.int32
U32 = mybir.dt.uint32
ALU = mybir.AluOpType
ACT = mybir.ActivationFunctionType
AX = mybir.AxisListType

P = 128
D = 1024
KD = D // P
T = 512
NT = T // P
EPS = 1e-6
BC = 256

GH, GDK, GDV, GRANK, GCHUNK = 4, 64, 128, 16, 64
GPAIRS = GH * GDK // P
GV_W = GH * GDV
NCHUNK = T // GCHUNK
GATE_TAU = 16.0
AH, AHD = 8, 64
BRANCHES = ((128, 1), (512, 4), (2048, 16))
RT = D // P
CONV = 4
LRU_C = 8.0
PH, PK, NKEYS = 8, 16, 128
HK = PH * PK
NEXP = NKEYS * NKEYS
NCH = NEXP // P
SPAN = 8
TB = 32
NEG = -3.0e38
CAND = []
_at = 0
for _a0, _na in ((0, 1), (1, 1), (2, 1), (3, 1), (4, 1), (5, 3), (8, 8)):
    CAND.append((_a0, _na, PK // (_a0 + 1), _at))
    _at += _na * (PK // (_a0 + 1))
NCAND = _at


def wait(eng, sem, value):
    if not (isinstance(value, int) and value <= 0):
        eng.wait_ge(sem, value)


class Scope:

    HELD = []

    @classmethod
    def reset(cls, nc):
        nc.clear_and_free_semaphores(list(cls.HELD))
        nc.all_engine_barrier()
        cls.HELD.clear()

    def __init__(self, nc, name):
        self.nc, self.name, self.stack = nc, name, ExitStack()

    def __enter__(self):
        self.stack.__enter__()
        return self

    def __exit__(self, *a):
        return self.stack.__exit__(*a)

    def sb(self, name, shape, dt=F32):
        return self.stack.enter_context(self.nc.sbuf_tensor(f"{self.name}_{name}", shape, dt))

    def at(self, name, place, shape, dt=F32):
        return self.nc.alloc_sbuf_tensor_at(f"{self.name}_{name}", shape, dt, offset=place)

    def ps(self, name, shape):
        return self.stack.enter_context(self.nc.psum_tensor(f"{self.name}_{name}", shape, F32))

    def sem(self, name):
        held = self.nc.alloc_semaphore(f"{self.name}_{name}")
        self.HELD.append(held)
        return held

    def block(self):
        return self.stack.enter_context(self.nc.Block())


class Chain:

    def __init__(self, eng, sem, start=0):
        self.eng, self.sem, self.n = eng, sem, start

    def link(self, ins):
        self.n = self.n + 1
        ins.then_inc(self.sem, 1)
        self.eng.wait_ge(self.sem, self.n)


class Norm:

    def __init__(self, nc, s, name, resid, gain, ident, bank, xn, xh, xl, after=None):
        self.nc, self.resid, self.gain, self.ident, self.ps, self.xh, self.xl = nc, resid, gain, ident, bank, xh, xl
        self.after = after
        self.xn = xn
        self.ss, self.ms, self.root, self.rs = (s.sb(f"{name}_{x}", [P, NT]) for x in ("ss", "ms", "root", "rs"))
        (self.squared, self.mean, self.rooted, self.chain, self.normed, self.turned, self.hi, self.ready) = (
            s.sem(f"{name}_{x}") for x in ("squared", "mean", "rooted", "chain", "normed", "turned", "hi", "ready"))

    def act(self, act):
        nc = self.nc
        if self.after:
            act.wait_ge(*self.after)
        for t in range(NT // 2):
            nc.scalar.activation(self.xn[:, t], self.resid[:, t], ACT.Square, accum_out=self.ss[:, t:t + 1]).then_inc(self.squared, 1)
        act.wait_ge(self.mean, 1)
        nc.scalar.activation(self.root[:], self.ms[:], ACT.Sqrt).then_inc(self.rooted, 1)
        for c in range(KD):
            act.wait_ge(self.turned, c + 1)
            nc.scalar.activation(self.xh[:, c], self.ps[:, c], ACT.Copy, scale=self.gain[:, c:c + 1]).then_inc(self.hi, 1)

    def dve(self, dve):
        nc = self.nc
        if self.after:
            dve.wait_ge(*self.after)
        for t in range(NT // 2, NT):
            nc.vector.tensor_tensor_reduce(out=self.xn[:, t], in0=self.resid[:, t], in1=self.resid[:, t], scale=1.0, scalar=0.0,
                                           op0=ALU.mult, op1=ALU.add, accum_out=self.ss[:, t:t + 1]).then_inc(self.squared, 1)
        dve.wait_ge(self.squared, NT)
        nc.vector.tensor_scalar(self.ms[:], self.ss[:], 1.0 / D, EPS, ALU.mult, ALU.add).then_inc(self.mean, 1)
        dve.wait_ge(self.rooted, 1)
        nc.vector.reciprocal(self.rs[:], self.root[:]).then_inc(self.chain, 1)
        dve.wait_ge(self.chain, 1)
        for t in range(NT):
            nc.vector.tensor_scalar(self.xn[:, t], self.resid[:, t], self.rs[:, t:t + 1], None, ALU.mult).then_inc(self.normed, 1)
        for c in range(KD):
            dve.wait_ge(self.hi, c + 1)
            nc.vector.scalar_tensor_tensor(self.xl[:, c], self.ps[:, c], self.gain[:, c:c + 1], self.xh[:, c].bitcast(F32),
                                           ALU.mult, ALU.subtract).then_inc(self.ready, 1)

    def pe(self, pe):
        for t in range(NT):
            pe.wait_ge(self.normed, t + 1)
            for c in range(KD):
                last = self.nc.tensor.transpose(self.ps[:, c, t * P:(t + 1) * P], self.xn[:, t, c * P:(c + 1) * P], self.ident[:])
                if t == NT - 1:
                    last.then_inc(self.turned, 1)


class SplitRows:

    def __init__(self, nc, s, name, rows, ident, bank, xh, xl):
        self.nc, self.rows, self.ident, self.ps, self.xh, self.xl = nc, rows, ident, bank, xh, xl
        self.turned, self.hi, self.ready = (s.sem(f"{name}_{x}") for x in ("turned", "hi", "ready"))

    def pe(self, pe):
        for c in range(KD):
            for t in range(NT):
                last = self.nc.tensor.transpose(self.ps[:, c, t * P:(t + 1) * P], self.rows[:, t, c * P:(c + 1) * P], self.ident[:])
            last.then_inc(self.turned, 1)

    def act(self, act):
        for c in range(KD):
            act.wait_ge(self.turned, c + 1)
            self.nc.scalar.activation(self.xh[:, c], self.ps[:, c], ACT.Copy).then_inc(self.hi, 1)

    def dve(self, dve):
        for c in range(KD):
            dve.wait_ge(self.hi, c + 1)
            self.nc.vector.tensor_tensor(self.xl[:, c], self.ps[:, c], self.xh[:, c].bitcast(F32), ALU.subtract).then_inc(self.ready, 1)


class Stream:

    def __init__(self, nc, s):
        self.nc = nc
        self.raw = s.sb("w_raw", [P, 2, KD * BC])
        self.wh = s.sb("w_hi", [P, 2, KD * BC], F32R)
        self.wl = s.sb("w_lo", [P, 2, KD * BC], F32R)
        self.loaded = [s.sem(f"w_loaded{k}") for k in range(2)]
        self.high, self.low, self.used = s.sem("w_high"), s.sem("w_low"), s.sem("w_used")

    def load(self, sp, n, k, src):
        wait(sp, self.low, n - 1)
        dst = self.raw[:, k]
        if len(src.shape) == 3:
            dst = dst.rearrange("p (a d) -> p a d", a=2)
        sp.dma_start(dst, src).then_inc(self.loaded[k], 16)

    def split_high(self, act, n, k):
        act.wait_ge(self.loaded[k], (n - k) * 8 + 16)
        wait(act, self.used, n - 1)
        self.nc.scalar.activation(self.wh[:, k], self.raw[:, k], ACT.Copy).then_inc(self.high, 1)

    def split_low(self, pool, n, k):
        pool.wait_ge(self.high, n + 1)
        self.nc.gpsimd.tensor_tensor(self.wl[:, k], self.raw[:, k], self.wh[:, k].bitcast(F32), ALU.subtract).then_inc(self.low, 1)

    def all_low(self, pool, count):
        with pool.Fori(0, count // 2) as r:
            for k in range(2):
                self.split_low(pool, r * 2 + k, k)


def three_pass(nc, out, lh, ll, rh, rl, first, last):
    nc.tensor.matmul(out, lh, rh, start=first, stop=False)
    nc.tensor.matmul(out, lh, rl, start=False, stop=False)
    return nc.tensor.matmul(out, ll, rh, start=False, stop=last)


def block_products(nc, w, k, xh, xl, ps, by_column, before=None):
    wh = w.wh[:, k].rearrange("p (k c) -> p k c", k=KD)
    wl = w.wl[:, k].rearrange("p (k c) -> p k c", k=KD)
    if by_column:
        for c in range(2):
            for d in range(KD):
                if before and c == 0:
                    before(d)
                cs = slice(c * P, (c + 1) * P)
                last = three_pass(nc, ps[:, c], wh[:, d, cs], wl[:, d, cs], xh[:, d], xl[:, d], d == 0, d == KD - 1)
    else:
        for t in range(NT):
            ts, half = slice(t * P, (t + 1) * P), slice((t % 2) * BC, (t % 2 + 1) * BC)
            for d in range(KD):
                if before and t == 0:
                    before(d)
                last = three_pass(nc, ps[:, t // 2, half], xh[:, d, ts], xl[:, d, ts], wh[:, d], wl[:, d],
                                  d == 0, d == KD - 1)
    return last


class Project:

    def __init__(self, nc, s, name, w, base, dram, count, bank, xh, xl, ready, dest, by_column, add=False):
        self.nc, self.w, self.base, self.dram, self.count, self.ps = nc, w, base, dram, count, bank
        self.xh, self.xl, self.ready, self.dest, self.by_column, self.add = xh, xl, ready, dest, by_column, add
        self.taken = s.sem(f"{name}_taken")

    def blocks(self, eng, body, peel=True):
        if peel:
            body(0)
        if self.count > 2 or not peel:
            with eng.Fori(1 if peel else 0, self.count // 2) as r:
                body(r)

    def sp(self, sp):
        self.blocks(sp, lambda r: [self.w.load(sp, r * 2 + k + self.base, k, self.dram[r * 2 + k]) for k in range(2)])

    def act(self, act):
        self.blocks(act, lambda r: [self.w.split_high(act, r * 2 + k + self.base, k) for k in range(2)])

    def dve(self, dve):
        nc = self.nc

        def body(r):
            for k in range(2):
                n = r * 2 + k
                dve.wait_ge(self.w.used, n + self.base + 1)
                src = self.ps[:, 2 * k:2 * k + 2]
                if self.by_column:
                    nc.vector.tensor_copy(self.dest[:, bass.ds(n * 2, 2)], src).then_inc(self.taken, 1)
                else:
                    out = self.dest[:, :, bass.ds(n * BC, BC)]
                    src = src.rearrange("p a (b c) -> p (a b) c", b=2)
                    if self.add:
                        nc.vector.tensor_tensor(out, src, out, ALU.add).then_inc(self.taken, 1)
                    else:
                        nc.vector.tensor_copy(out, src).then_inc(self.taken, 1)
        self.blocks(dve, body)

    def pe(self, pe):
        def body(r):
            for k in range(2):
                n = r * 2 + k
                pe.wait_ge(self.w.low, n + self.base + 1)
                wait(pe, self.taken, n - 1)
                before = (lambda d: pe.wait_ge(self.ready, d + 1)) if isinstance(n, int) and n == 0 and self.ready else None
                block_products(self.nc, self.w, k, self.xh, self.xl, self.ps[:, 2 * k:2 * k + 2], self.by_column,
                               before).then_inc(self.w.used, 1)
        self.blocks(pe, body)


class Queries:

    def __init__(self, nc, s, w, base, dram, keys_dram, bank, xh, xl, ready, keys, q, scores):
        self.nc, self.w, self.base, self.dram, self.keys_dram, self.ps = nc, w, base, dram, keys_dram, bank
        self.xh, self.xl, self.ready, self.keys, self.q, self.scores = xh, xl, ready, keys, q, scores
        self.keys_in, self.q_there, self.s_done, self.s_taken = (s.sem(x) for x in ("keys_in", "q_there", "s_done", "s_taken"))

    def blocks(self, eng, body):
        body(0)
        with eng.Fori(1, PH // 2) as r:
            body(r)

    def sp(self, sp, keys_after):
        def body(r):
            for k in range(2):
                self.w.load(sp, r * 2 + k + self.base, k, self.dram[r * 2 + k])
            if isinstance(r, int):
                sp.wait_ge(*keys_after)
                sp.dma_start(self.keys[:], self.keys_dram).then_inc(self.keys_in, 16)
        self.blocks(sp, body)

    def act(self, act):
        self.blocks(act, lambda r: [self.w.split_high(act, r * 2 + k + self.base, k) for k in range(2)])

    def dve(self, dve):
        nc = self.nc

        def take_scores(n):
            dve.wait_ge(self.s_done, n + 1)
            for p in range(2):
                last = nc.vector.tensor_copy(self.scores[:, :, bass.ds(n * 2 + p, 1)].rearrange("p t o c -> p t (o c)"),
                                             self.ps[:, 4 + p].rearrange("p (t c) -> p t c", c=NKEYS))
            last.then_inc(self.s_taken, 1)

        def body(r):
            for k in range(2):
                n = r * 2 + k
                dve.wait_ge(self.w.used, n + self.base + 1)
                wait(dve, self.s_done, n - 1)
                nc.vector.tensor_copy(self.q[:, k], self.ps[:, 2 * k:2 * k + 2]).then_inc(self.q_there, 1)
                if not (isinstance(n, int) and n == 0):
                    take_scores(n - 1)
        self.blocks(dve, body)
        take_scores(PH - 1)
        dve.wait_ge(self.s_taken, PH)

    def pe(self, pe):
        nc = self.nc

        def score(n, k):
            pe.wait_ge(self.q_there, n + 1)
            wait(pe, self.s_taken, n)
            for p in range(2):
                kp = self.keys[:, bass.ds((n * 2 + p) * NKEYS, NKEYS)]
                for t in range(NT):
                    ts = slice(t * P, (t + 1) * P)
                    last = nc.tensor.matmul(self.ps[:, 4 + p, ts], self.q[:, k, p, ts], kp, start=True, stop=True)
            last.then_inc(self.s_done, 1)

        def body(r):
            for k in range(2):
                n = r * 2 + k
                first = isinstance(n, int) and n == 0
                pe.wait_ge(self.w.low, n + self.base + 1)
                wait(pe, self.q_there, n - 1)
                before = (lambda d: pe.wait_ge(self.ready, d + 1)) if first else None
                block_products(nc, self.w, k, self.xh, self.xl, self.ps[:, 2 * k:2 * k + 2], True, before).then_inc(self.w.used, 1)
                if first:
                    pe.wait_ge(self.keys_in, 16)
                else:
                    score(n - 1, 1 - k)
        self.blocks(pe, body)

    def pe_last(self, pe):
        nc = self.nc
        pe.wait_ge(self.q_there, PH)
        pe.wait_ge(self.s_taken, PH - 1)
        for p in range(2):
            kp = self.keys[:, ((PH - 1) * 2 + p) * NKEYS:(PH * 2 - 1 + p) * NKEYS]
            for t in range(NT):
                ts = slice(t * P, (t + 1) * P)
                last = nc.tensor.matmul(self.ps[:, 4 + p, ts], self.q[:, 1, p, ts], kp, start=True, stop=True)
        last.then_inc(self.s_done, 1)


ROOM = 28000

PAIRS = NCH // 2
LEAD = 8
PERIOD = (PAIRS - LEAD) // NT
BATCH = 4
NB = P // BATCH
GB = TB // BATCH
POINTS = 4
SPREAD = [POINTS + b * (PERIOD - 1) * POINTS // NB for b in range(NB)]
EARLY = [POINTS + b * 5 // 4 for b in range(NB)]


def batches(plan, first, last):
    return [b for b in range(NB) if first * POINTS <= plan[b] < (last + 1) * POINTS]


OH = 3
CREDIT = 2


class Room:

    def __init__(self, nc, s, words):
        self.s, self.words, self.next = s, words, 0
        self.base = nc.lookup_mloc(s.sb("room", [P, words])).addr

    def part(self, name, first, shape, dt=F32):
        assert first + math.prod(shape[1:]) <= self.words, (name, first, shape)
        return self.s.at(name, self.base + first * 4, shape, dt)

    def sb(self, name, shape, dt=F32):
        first = self.next
        self.next = first + -(-math.prod(shape[1:]) // 8) * 8
        return self.part(name, first, shape, dt)


class Up:

    STORE_LAG = 4
    GATE_LAG = 3

    def __init__(self, nc, s, w, base, uT, h_dram, g_dram, consts, bank, xh, xl, scores, gst, room):
        self.nc, self.w, self.base, self.uT, self.h_dram, self.g_dram = nc, w, base, uT, h_dram, g_dram
        self.ident, self.iota, self.ps, self.xh, self.xl, self.scores = consts["ident"], consts["iota"], bank, xh, xl, scores
        self.gst = gst
        room.next = 16384
        self.hs = room.sb("h_out", [P, 2, 2, T])
        at_work = room.next
        self.work = room.sb("work", [P, 2 * PH, NKEYS])
        self.cv = room.part("cand_sum", at_work, [P, PH, NCAND])
        self.ci = room.part("cand_id", at_work + PH * NCAND, [P, PH, NCAND])
        self.pick = room.part("pick", at_work + 2 * PH * NCAND, [P, PK, NCAND])
        self.top = room.sb("top", [P, 2 * PH, PK])
        self.topi = room.sb("topi", [P, 2 * PH, PK], U32)
        self.topf = room.sb("topf", [P, 2 * PH, PK])
        self.best = room.sb("best", [P, PH, PK])
        self.posi = room.sb("posi", [P, PH, PK], U32)
        self.posf = room.sb("posf", [P, PH, PK])
        self.idf = room.sb("idf", [P, HK])
        self.idi = room.sb("idi", [P, 3, HK], I32)
        self.ijg = room.sb("ijg", [P, 3, HK])
        self.den = room.sb("den", [P, PH])
        self.tick = room.sb("tick", [P, 1])
        self.here = room.sb("here", [P, 3, P])
        self.split = room.sb("gate_split", [P, 2, P])
        self.ghi = room.sb("gate_hi", [P, P], F32R)
        self.oh = room.sb("onehot", [P, OH, BATCH, 3, P], F32R)
        (self.h_there, self.chain, self.diff, self.exped, self.chosen, self.turned, self.tiles, self.onehots, self.g_done,
         self.g_there) = (
            s.sem(x) for x in ("h_there", "choice_chain", "diff", "exped", "chosen", "turned", "tiles", "onehots", "g_done", "g_there"))
        self.h_stored = [s.sem(f"h_stored{k}") for k in range(2)]
        self.g_stored = [s.sem(f"g_stored{k}") for k in range(2)]

    def store_hidden(self, sp, n, k):
        sp.wait_ge(self.h_there, n * 2 + 2)
        sp.dma_start(self.h_dram[n], self.hs[:, k].rearrange("p a t -> p (a t)")).then_inc(self.h_stored[k], 16)

    def store_gates(self, sp, c, done):
        for b in [n // GB for n in done if n % GB == GB - 1]:
            sp.wait_ge(self.g_there, c * NB + ((b + 1) * GB + CREDIT))
            sp.dma_start(self.g_dram[c * (P // TB) + b], self.gst[:, b % 2].rearrange("p i t -> p (i t)")).then_inc(
                self.g_stored[b % 2], 16)

    def sp(self, sp):
        lag = self.STORE_LAG
        for k in range(2):
            sp.sem_inc(self.g_stored[k], 16)
        for n in range(LEAD):
            self.w.load(sp, n + self.base, n % 2, self.uT[n])
            if n >= lag:
                self.store_hidden(sp, n - lag, n % 2)

        def period(c):
            for p in range(PERIOD):
                n = c * PERIOD + LEAD + p
                self.w.load(sp, n + self.base, p % 2, self.uT[n])
                self.store_hidden(sp, n - lag, p % 2)
                q = p - self.GATE_LAG
                if q >= 0:
                    self.store_gates(sp, c, batches(EARLY if isinstance(c, int) and c == NT - 1 else SPREAD, q, q))
                elif not (isinstance(c, int) and c == 0):
                    self.store_gates(sp, c - 1, batches(SPREAD, PERIOD + q, PERIOD + q))
        period(0)
        with sp.Fori(1, NT - 1) as c:
            period(c)
        period(NT - 1)

    def act_after(self, act, n, k, c, done, first=False):
        nc = self.nc
        act.wait_ge(self.w.used, n + self.base + 1)
        if not first:
            act.wait_ge(self.h_stored[k], (n - k) * 8)
        for a in range(2):
            nc.scalar.activation(self.hs[:, k, a], self.ps[:, 2 * k + a], ACT.Gelu_apprx_tanh).then_inc(self.h_there, 1)
        for b in done:
            t0, kb = b % GB * BATCH, b // GB % 2
            act.wait_ge(self.g_done, c * NB + (b + 1 + CREDIT))
            if t0 == 0:
                act.wait_ge(self.g_stored[kb], c * (16 * NB // GB // 2) + (16 * (b // GB // 2) + 16))
            nc.scalar.activation(self.gst[:, kb, :, t0:t0 + BATCH].rearrange("p i t -> p t i"),
                                 self.ps[:, 4 + b % 2].rearrange("p (t i) -> p t i", t=BATCH), ACT.Copy).then_inc(self.g_there, 1)

    def exponentials(self, act, c):
        act.wait_ge(self.diff, c + 1)
        self.nc.scalar.activation(self.best[:], self.best[:], ACT.Exp).then_inc(self.exped, 1)

    def act(self, act):
        act.sem_inc(self.g_there, CREDIT)
        for n in range(LEAD):
            self.w.split_high(act, n + self.base, n % 2)
            if n >= 2:
                self.act_after(act, n - 2, n % 2, 0, [], first=n < 4)

        def period(c, spread):
            for p in range(PERIOD):
                n = c * PERIOD + LEAD + p
                self.w.split_high(act, n + self.base, p % 2)
                if isinstance(c, int) and c == 0 and p == 0:
                    self.exponentials(act, 0)
                if p >= 1:
                    self.act_after(act, n - 2, p % 2, c, batches(spread, p - 1, p - 1))
                elif isinstance(c, int) and c == 0:
                    self.act_after(act, n - 2, p % 2, 0, [])
                else:
                    self.act_after(act, n - 2, p % 2, c - 1, batches(SPREAD, PERIOD - 1, PERIOD - 1))
                if p == PERIOD - 1 and spread is SPREAD:
                    self.exponentials(act, c + 1)
        period(0, SPREAD)
        with act.Fori(1, NT - 1) as c:
            period(c, SPREAD)
        period(NT - 1, EARLY)

    def act_rest(self, act, k):
        self.act_after(act, PAIRS - 2 + k, k, NT - 1, [])

    STEPS = 4 * PH + 2
    LINKS = 1 + 2 * PH * 5 + 3 + PH * 9 + 3 + 2

    def choice(self, dve, c):
        nc, links = self.nc, [0]

        def link(ins):
            links[0] += 1
            ins.then_inc(self.chain, 1)
            dve.wait_ge(self.chain, c * self.LINKS + links[0])
            nc.vector.memset(self.tick[:], 0.0)

        def best_of(values, best, at):
            for v in range(2):
                e = slice(8 * v, 8 * v + 8)
                link(nc.vector.max(best[:, e], values))
                link(nc.vector.max_index(at[:, e], best[:, e], values))
                if v == 0:
                    link(nc.vector.match_replace(values, best[:, e], values, NEG))

        def half(a):
            if a == 0:
                link(nc.vector.tensor_copy(self.work[:], self.scores[:, bass.ds(c, 1)].rearrange("p o a n -> p (o a) n")))
            best_of(self.work[:, a], self.top[:, a], self.topi[:, a])

        def sums():
            link(nc.vector.tensor_copy(self.topf[:], self.topi[:]))
            tf = self.topf[:].rearrange("p (h o) k -> p h o k", o=2)
            tv = self.top[:].rearrange("p (h o) k -> p h o k", o=2)
            link(nc.vector.tensor_scalar(tf[:, :, 0], tf[:, :, 0], float(NKEYS), None, ALU.mult))
            for src, dst in ((tv, self.cv), (tf, self.ci)):
                for a0, na, nb, at in CAND:
                    out = dst[:, :, at:at + na * nb].rearrange("p h (a b) -> p h a b", a=na)
                    one = src[:, :, 0, a0:a0 + na].unsqueeze(3).to_broadcast([P, PH, na, nb])
                    two = src[:, :, 1, 0:nb].unsqueeze(2).to_broadcast([P, PH, na, nb])
                    last = nc.vector.tensor_tensor(out, one, two, ALU.add)
            link(last)

        def head(h):
            best_of(self.cv[:, h], self.best[:, h], self.posi[:, h])
            link(nc.vector.tensor_copy(self.posf[:, h], self.posi[:, h]))

        def experts(h):
            pos = self.posf[:, h].unsqueeze(2).to_broadcast([P, PK, NCAND])
            at = self.iota[:, 0:NCAND].unsqueeze(1).to_broadcast([P, PK, NCAND])
            ids = self.ci[:, h].unsqueeze(1).to_broadcast([P, PK, NCAND])
            link(nc.vector.tensor_tensor(self.pick[:], pos, at, ALU.is_equal))
            link(nc.vector.tensor_tensor(self.pick[:], self.pick[:], ids, ALU.mult))
            link(nc.vector.tensor_reduce(self.idf[:, h * PK:(h + 1) * PK], self.pick[:], AX.X, ALU.add))

        def difference():
            first = self.best[:, :, 0:1].to_broadcast([P, PH, PK - 1])
            link(nc.vector.tensor_tensor(self.best[:, :, 1:], self.best[:, :, 1:], first, ALU.subtract))
            nc.vector.memset(self.best[:, :, 0:1], 0.0).then_inc(self.diff, 1)
            link(nc.vector.tensor_copy(self.idi[:, 0], self.idf[:]))
            nc.vector.tensor_scalar(self.idi[:, 1], self.idi[:, 0], 7, None, ALU.arith_shift_right)
            link(nc.vector.tensor_scalar(self.idi[:, 2], self.idi[:, 0], NKEYS - 1, None, ALU.bitwise_and))
            nc.vector.tensor_copy(self.ijg[:, 0:2], self.idi[:, 1:3])

        def end():
            dve.wait_ge(self.exped, c + 1)
            link(nc.vector.tensor_reduce(self.den[:], self.best[:], AX.X, ALU.add))
            link(nc.vector.reciprocal(self.den[:], self.den[:]))
            nc.vector.tensor_tensor(self.ijg[:, 2].rearrange("p (h k) -> p h k", h=PH), self.best[:],
                                    self.den[:].unsqueeze(2).to_broadcast([P, PH, PK]), ALU.mult).then_inc(self.chosen, 1)
            assert links[0] == self.LINKS, links[0]

        def step(n):
            if n < 2 * PH:
                half(n)
            elif n == 2 * PH:
                sums()
            elif n <= 4 * PH:
                (head, experts)[(n - 1) % 2]((n - 1 - 2 * PH) // 2)
            else:
                difference()

        return step, end

    def dve(self, dve):
        nc = self.nc
        step, end = self.choice(dve, 0)
        for n in range(self.STEPS):
            step(n)
        end()

        def period(c):
            last_tile = isinstance(c, int)
            dve.wait_ge(self.turned, c + 1)
            nc.vector.tensor_copy(self.here[:], self.ps[:, 6, 0:3 * P].rearrange("p (v t) -> p v t", v=3)).then_inc(self.tiles, 1)
            dve.wait_ge(self.tiles, c * 3 + 1)
            nc.vector.tensor_copy(self.ghi[:], self.here[:, 2]).then_inc(self.tiles, 1)
            dve.wait_ge(self.tiles, c * 3 + 2)
            nc.vector.tensor_copy(self.split[:, 0], self.ghi[:].bitcast(F32))
            nc.vector.tensor_tensor(self.split[:, 1], self.here[:, 2], self.ghi[:].bitcast(F32), ALU.subtract).then_inc(self.tiles, 1)
            dve.wait_ge(self.tiles, c * 3 + 3)
            step, end = (None, None) if last_tile else self.choice(dve, c + 1)
            for b in range(NB):
                dve.wait_ge(self.g_done, c * NB + (b + 1 + CREDIT - (OH if b >= 2 else 2)))
                toks = slice(b * BATCH, (b + 1) * BATCH)
                o = self.oh[:, b % OH]
                nc.vector.tensor_tensor(o[:, :, 0], self.here[:, 1, toks].unsqueeze(2).to_broadcast([P, BATCH, P]),
                                        self.iota[:].unsqueeze(1).to_broadcast([P, BATCH, P]), ALU.is_equal)
                for t in range(BATCH):
                    tok = b * BATCH + t
                    last = nc.vector.scalar_tensor_tensor(
                        o[:, t, 1:3], self.iota[:].unsqueeze(1).to_broadcast([P, 2, P]), self.here[:, 0, tok:tok + 1],
                        self.split[:, :, tok:tok + 1].to_broadcast([P, 2, P]), ALU.is_equal, ALU.mult)
                last.then_inc(self.onehots, 1)
                if not last_tile and b < NB - 2:
                    for n in range(b * self.STEPS // (NB - 2), (b + 1) * self.STEPS // (NB - 2)):
                        step(n)
            if not last_tile:
                end()
        with dve.Fori(0, NT - 1) as c:
            period(c)
        period(NT - 1)

    def pair_products(self, pe, n, k, at_point=None, first=False):
        w, nc = self.w, self.nc
        pe.wait_ge(w.low, n + self.base + 1)
        if not first:
            pe.wait_ge(self.h_there, (n - 1) * 2)
        wh = w.wh[:, k].rearrange("p (a k e) -> p a k e", a=2, k=KD)
        wl = w.wl[:, k].rearrange("p (a k e) -> p a k e", a=2, k=KD)
        for a in range(2):
            for d in range(KD):
                last = three_pass(nc, self.ps[:, 2 * k + a], wh[:, a, d], wl[:, a, d], self.xh[:, d], self.xl[:, d],
                                  d == 0, d == KD - 1)
                if at_point and d % (2 * KD // POINTS) == KD // POINTS - 1:
                    at_point((a * KD + d) // (2 * KD // POINTS))
        last.then_inc(w.used, 1)

    def turn(self, pe, c):
        pe.wait_ge(self.chosen, c + 1)
        for v in range(3):
            last = self.nc.tensor.transpose(self.ps[:, 6, v * P:(v + 1) * P], self.ijg[:, v], self.ident[:])
        last.then_inc(self.turned, 1)

    def pe(self, pe, behind_first):
        nc = self.nc
        pe.sem_inc(self.g_done, CREDIT)
        for n in range(LEAD):
            self.pair_products(pe, n, n % 2, (lambda j: behind_first() if j == 2 else None) if n == 0 else None,
                               first=n < 2)

        def batch(c, b):
            pe.wait_ge(self.onehots, c * NB + (b + 1))
            pe.wait_ge(self.g_there, c * NB + (b + CREDIT - 1))
            for t in range(BATCH):
                o, out = self.oh[:, b % OH, t], self.ps[:, 4 + b % 2, t * P:(t + 1) * P]
                nc.tensor.matmul(out, o[:, 0], o[:, 1], start=True, stop=False)
                last = nc.tensor.matmul(out, o[:, 0], o[:, 2], start=False, stop=True)
            last.then_inc(self.g_done, 1)

        def period(c, spread):
            def at_point(p, j):
                if p == 0 and j == 1:
                    self.turn(pe, c)
                for b in range(NB):
                    if spread[b] == p * POINTS + j:
                        batch(c, b)
            for p in range(PERIOD):
                self.pair_products(pe, c * PERIOD + LEAD + p, p % 2, lambda j: at_point(p, j))
        with pe.Fori(0, NT - 1) as c:
            period(c, SPREAD)
        period(NT - 1, EARLY)


class Down:

    BODY = 4

    def __init__(self, nc, s, w, base, v, up, h_dram, g_dram, bank, resid, hin, gin, a, ah, al):
        self.nc, self.w, self.base, self.up, self.h_dram, self.ps = nc, w, base, up, h_dram, bank
        self.resid, self.hin, self.gin, self.a, self.ah, self.al = resid, hin, gin, a, ah, al
        self.v_rows = v.rearrange("(n a j) d -> n j a d", a=2, j=P)
        self.g_rows = g_dram.rearrange("b j x -> j b x")
        self.h_in = [s.sem(f"h_in{k}") for k in range(4)]
        self.g_in = [s.sem(f"g_in{k}") for k in range(2)]
        self.a_there, self.a_high, self.a_low, self.added = (s.sem(x) for x in ("a_there", "a_high", "a_low", "added"))

    def bodies(self, eng, body):
        body(0)
        with eng.Fori(1, PAIRS // self.BODY) as r:
            body(r)

    def sp(self, sp):
        up, lag = self.up, self.up.STORE_LAG

        def body(r):
            peeled = isinstance(r, int)
            for q in range(self.BODY):
                n = r * self.BODY + q
                self.w.load(sp, n + self.base, q % 2, self.v_rows[n])
                if peeled:
                    up.store_hidden(sp, PAIRS - lag + q, q % 2)
                    if q == 0:
                        for k in range(2):
                            sp.wait_ge(up.g_stored[k], 16 + 16 * (T // TB // 2))
                            sp.wait_ge(up.h_stored[k], 16 * (PAIRS - lag) // 2)
                if q % 2 == 0:
                    kg = q // 2
                    if not peeled:
                        sp.wait_ge(self.a_there, (r - 1) * (2 * self.BODY) + 4 * (kg + 1))
                    sp.dma_start(self.gin[:, kg].rearrange("p b i t -> p b (i t)"),
                                 self.g_rows[:, :, bass.ds(n * (2 * TB), 4 * TB)]).then_inc(self.g_in[kg], 16)
                if not peeled:
                    sp.wait_ge(self.a_there, (r - 1) * (2 * self.BODY) + 2 * (q + 1))
                sp.dma_start(self.hin[:, q].rearrange("p a t -> p (a t)"), self.h_dram[n]).then_inc(self.h_in[q], 16)
        body(0)
        for k in range(2):
            sp.wait_ge(up.h_stored[k], 16 * PAIRS // 2)
        with sp.Fori(1, PAIRS // self.BODY) as r:
            body(r)

    def act(self, act):
        def body(r):
            peeled = isinstance(r, int)
            for q in range(self.BODY):
                n = r * self.BODY + q
                self.w.split_high(act, n + self.base, q % 2)
                if peeled and q < 2:
                    self.up.act_rest(act, q)
                for e in range(2):
                    act.wait_ge(self.a_there, n * 2 + e + 1)
                    self.nc.scalar.activation(self.ah[:, (2 * q + e) % 4], self.a[:, (2 * q + e) % 4], ACT.Copy).then_inc(self.a_high, 1)
        self.bodies(act, body)

    def dve(self, dve):
        nc = self.nc

        def low(m, q):
            dve.wait_ge(self.a_high, m + 1)
            nc.vector.tensor_tensor(self.al[:, q % 4], self.a[:, q % 4], self.ah[:, q % 4].bitcast(F32),
                                    ALU.subtract).then_inc(self.a_low, 1)

        def body(r):
            peeled = isinstance(r, int)
            for q in range(2 * self.BODY):
                m = r * (2 * self.BODY) + q
                dve.wait_ge(self.h_in[q // 2], r * 16 + 16)
                dve.wait_ge(self.g_in[q // 4], r * 16 + 16)
                if not (peeled and q < 4):
                    dve.wait_ge(self.a_low, m - 3)
                nc.vector.tensor_tensor(self.a[:, q % 4].rearrange("p (b t) -> p b t", t=TB),
                                        self.hin[:, q // 2, q % 2].rearrange("p (b t) -> p b t", t=TB),
                                        self.gin[:, q // 4, :, q % 4], ALU.mult).then_inc(self.a_there, 1)
                if not (peeled and q == 0):
                    low(m - 1, (q - 1) % 8)
        self.bodies(dve, body)
        low(NCH - 1, 7)
        for t in range(NT):
            dve.wait_ge(self.w.used, self.base + PAIRS)
            nc.vector.tensor_tensor(self.resid[:, t].rearrange("p (a c) -> p a c", a=2), self.ps[:, 2 * t:2 * t + 2],
                                    self.resid[:, t].rearrange("p (a c) -> p a c", a=2), ALU.add).then_inc(self.added, 1)

    def pe(self, pe):
        def body(r, first, last_set):
            for q in range(self.BODY):
                n = r * self.BODY + q
                pe.wait_ge(self.w.low, n + self.base + 1)
                wh = self.w.wh[:, q % 2].rearrange("p (a d) -> p a d", a=2)
                wl = self.w.wl[:, q % 2].rearrange("p (a d) -> p a d", a=2)
                for e in range(2):
                    pe.wait_ge(self.a_low, n * 2 + e + 1)
                    k = (2 * q + e) % 4
                    start, stop = first and q == 0 and e == 0, last_set and q == self.BODY - 1 and e == 1
                    for t in (2, 3, 0, 1):
                        if start and t == 0:
                            pe.wait_ge(self.up.h_there, NCH)
                        ts = slice(t * P, (t + 1) * P)
                        for c in range(2):
                            cs = slice(c * T, (c + 1) * T)
                            last = three_pass(self.nc, self.ps[:, 2 * t + c], self.ah[:, k, ts], self.al[:, k, ts],
                                              wh[:, e, cs], wl[:, e, cs], start, stop)
                last.then_inc(self.w.used, 1)
        pe.wait_ge(self.up.g_there, T // BATCH + CREDIT)
        body(0, True, False)
        with pe.Fori(1, PAIRS // self.BODY - 1) as r:
            body(r, False, False)
        body(PAIRS // self.BODY - 1, False, True)


class Recurrent:

    def __init__(self, nc, s, w, base, A, bank, xh, xl, ready, gxT, xc, rg, ig, a, yh, yl, wr, wi):
        self.nc, self.w, self.base, self.A, self.ps, self.xh = nc, w, base, A, bank, xh
        self.xl, self.in_ready, self.gxT, self.xc, self.rg, self.ig = xl, ready, gxT, xc, rg, ig
        self.a, self.yh, self.yl, self.wr, self.wi = a, yh, yl, wr, wi
        self.cw, self.vec, self.sp8 = s.sb("conv_w", [P, RT, CONV]), s.sb("vec", [P, 4, RT]), s.sb("sp8", [P, 8, RT])
        (self.loaded, self.chain, self.conved, self.gated, self.g_done, self.exps, self.lam_abs, self.lam_exp, self.sp_there,
         self.rooted, self.q_there, self.gelus, self.y_there, self.hi, self.ready, self.taken) = (s.sem(f"rec_{x}") for x in (
             "loaded", "chain", "conved", "gated", "g_done", "exps", "lam_abs", "lam_exp", "sp_there", "rooted", "q_there",
             "gelus", "y_there", "hi", "ready", "taken"))

    BLOCKS = 2 * D // BC
    HALF = BLOCKS // 2

    def sp(self, sp):
        A = self.A
        for n in range(2):
            self.w.load(sp, n + self.base, n, A["w_c_in"][n])
        for dst, src in ((self.wr[:], A["w_rgate"]), (self.wi[:], A["w_igate"]), (self.cw[:], A["conv_w"]),
                         (self.vec[:, 0], A["conv_b"]), (self.vec[:, 1], A["b_rgate"]), (self.vec[:, 2], A["b_igate"]),
                         (self.vec[:, 3], A["lam"])):
            sp.dma_start(dst, src).then_inc(self.loaded, 16)
        with sp.Fori(1, self.BLOCKS // 2) as r:
            for k in range(2):
                self.w.load(sp, r * 2 + k + self.base, k, A["w_c_in"][r * 2 + k])

    LOADED = 7 * 16

    def act(self, act):
        nc = self.nc
        act.wait_ge(self.loaded, self.LOADED)
        nc.scalar.activation(self.sp8[:, 0], self.vec[:, 3], ACT.Abs).then_inc(self.lam_abs, 1)
        act.wait_ge(self.lam_abs, 1)
        nc.scalar.activation(self.sp8[:, 1], self.sp8[:, 0], ACT.Exp, scale=-1.0).then_inc(self.lam_exp, 1)
        for n in range(self.BLOCKS):
            self.w.split_high(act, n + self.base, n % 2)
            for g in (2 * (n - 2), 2 * (n - 2) + 1):
                if 0 <= g < RT:
                    act.wait_ge(self.g_done, g + 1)
                    nc.scalar.activation(self.rg[:, g], self.ps[:, 4 + 2 * (g % 2)], ACT.Sigmoid, bias=self.vec[:, 1, g:g + 1])
                    nc.scalar.activation(self.ig[:, g], self.ps[:, 5 + 2 * (g % 2)], ACT.Sigmoid,
                                         bias=self.vec[:, 2, g:g + 1]).then_inc(self.gated, 1)
            if n == self.HALF + 1:
                act.wait_ge(self.sp_there, 1)
                act.wait_ge(self.gated, RT)
                for g in range(RT):
                    nc.scalar.activation(self.a[:, g], self.rg[:, g], ACT.Exp, scale=self.sp8[:, 6, g:g + 1]).then_inc(self.exps, 1)
                    nc.scalar.activation(self.rg[:, g], self.rg[:, g], ACT.Tanh, scale=self.sp8[:, 7, g:g + 1]).then_inc(self.exps, 1)
            if n == self.HALF + 2:
                for g in range(RT):
                    act.wait_ge(self.q_there, g + 1)
                    nc.scalar.activation(self.rg[:, g], self.gxT[:, g], ACT.Sqrt).then_inc(self.rooted, 1)
        for g in range(RT):
            act.wait_ge(self.taken, self.HALF + g // 2 + 1)
            nc.scalar.activation(self.gxT[:, RT + g], self.gxT[:, RT + g], ACT.Gelu_apprx_tanh).then_inc(self.gelus, 1)
            if g:
                self.high(act, g - 1)
        self.high(act, RT - 1)

    def high(self, act, g):
        act.wait_ge(self.y_there, g + 1)
        self.nc.scalar.activation(self.yh[:, g], self.a[:, g], ACT.Copy).then_inc(self.hi, 1)

    def dve(self, dve):
        nc = self.nc
        link = Chain(dve, self.chain).link
        x, sp8, vec, cw = self.gxT, self.sp8, self.vec, self.cw

        def take(n):
            k = n % 2
            dve.wait_ge(self.w.used, n + self.base + 1)
            nc.vector.tensor_copy(x[:, 2 * n:2 * n + 2], self.ps[:, 2 * k:2 * k + 2]).then_inc(self.taken, 1)
            dve.wait_ge(self.taken, n + 1)

        dve.wait_ge(self.loaded, self.LOADED)
        for n in range(self.HALF):
            take(n)
            for g in (2 * n, 2 * n + 1):
                link(nc.vector.tensor_scalar(self.xc[:, g], x[:, g], cw[:, g, 3:4], vec[:, 0, g:g + 1], ALU.mult, ALU.add))
                for k in (1, 2, 3):
                    ins = nc.vector.scalar_tensor_tensor(self.xc[:, g, k:], x[:, g, 0:T - k], cw[:, g, 3 - k:4 - k], self.xc[:, g, k:],
                                                         ALU.mult, ALU.add)
                    if k < 3:
                        link(ins)
                    else:
                        ins.then_inc(self.conved, 1)
            if n == 0:
                self.softplus(dve, link)
        take(self.HALF)
        take(self.HALF + 1)
        for g in range(RT):
            dve.wait_ge(self.exps, 2 * (g + 1))
            link(nc.vector.tensor_tensor(x[:, g], self.a[:, g], self.a[:, g], ALU.mult))
            nc.vector.scalar_tensor_tensor(x[:, g], x[:, g], 1.0, self.rg[:, g], ALU.add, ALU.mult).then_inc(self.q_there, 1)
            link(nc.vector.tensor_tensor(self.xc[:, g], self.xc[:, g], self.ig[:, g], ALU.mult))
        take(self.HALF + 2)
        for g in range(RT):
            if g == RT // 2:
                take(self.HALF + 3)
            dve.wait_ge(self.rooted, g + 1)
            link(nc.vector.tensor_tensor(self.xc[:, g], self.xc[:, g], self.rg[:, g], ALU.mult))
            link(nc.vector.tensor_tensor_scan(self.ig[:, g], self.a[:, g], self.xc[:, g], 0.0, ALU.mult, ALU.add))
        for g in range(RT):
            dve.wait_ge(self.gelus, g + 1)
            nc.vector.tensor_tensor(self.a[:, g], x[:, RT + g], self.ig[:, g], ALU.mult).then_inc(self.y_there, 1)
            if g:
                self.low(dve, g - 1)
        self.low(dve, RT - 1)

    def low(self, dve, g):
        dve.wait_ge(self.hi, g + 1)
        self.nc.vector.tensor_tensor(self.yl[:, g], self.a[:, g], self.yh[:, g].bitcast(F32), ALU.subtract).then_inc(self.ready, 1)

    def softplus(self, dve, link):
        nc, sp8 = self.nc, self.sp8
        dve.wait_ge(self.lam_exp, 1)
        e, z, z2, acc, tmp = (sp8[:, k] for k in range(1, 6))
        link(nc.vector.tensor_scalar(tmp, e, 2.0, None, ALU.add))
        link(nc.vector.reciprocal(tmp, tmp))
        link(nc.vector.tensor_tensor(z, e, tmp, ALU.mult))
        link(nc.vector.tensor_tensor(z2, z, z, ALU.mult))
        link(nc.vector.tensor_scalar(acc, z2, 1.0 / 17, 1.0 / 15, ALU.mult, ALU.add))
        for k in (13, 11, 9, 7, 5, 3, 1):
            link(nc.vector.tensor_tensor(acc, acc, z2, ALU.mult))
            link(nc.vector.tensor_scalar(acc, acc, 1.0 / k, None, ALU.add))
        link(nc.vector.tensor_tensor(acc, acc, z, ALU.mult))
        link(nc.vector.tensor_scalar(acc, acc, 2.0, None, ALU.mult))
        link(nc.vector.tensor_scalar(tmp, self.vec[:, 3], -1.0, 0.0, ALU.mult, ALU.max))
        link(nc.vector.tensor_tensor(acc, acc, tmp, ALU.add))
        link(nc.vector.tensor_scalar(sp8[:, 6], acc, -LRU_C, None, ALU.mult))
        nc.vector.tensor_scalar(sp8[:, 7], acc, LRU_C, None, ALU.mult).then_inc(self.sp_there, 1)

    def pe(self, pe):
        nc = self.nc

        def gates(g):
            pe.wait_ge(self.conved, g + 1)
            wait(pe, self.gated, g - 1)
            nc.tensor.matmul(self.ps[:, 4 + 2 * (g % 2)], self.wr[:, g], self.xc[:, g], start=True, stop=True)
            nc.tensor.matmul(self.ps[:, 5 + 2 * (g % 2)], self.wi[:, g], self.xc[:, g], start=True, stop=True).then_inc(self.g_done, 1)

        for n in range(self.BLOCKS):
            pe.wait_ge(self.w.low, n + self.base + 1)
            wait(pe, self.taken, n - 1)
            before = (lambda d: pe.wait_ge(self.in_ready, d + 1)) if n == 0 else None
            block_products(nc, self.w, n % 2, self.xh, self.xl, self.ps[:, 2 * (n % 2):2 * (n % 2) + 2], True,
                           before).then_inc(self.w.used, 1)
            for g in (2 * (n - 1), 2 * (n - 1) + 1):
                if 0 <= g < RT:
                    gates(g)


def gla_stage(nc, name, consts, qkT, gv, gg, glrT, w_alpha, b_alpha, gain, mixed):
    scan_mask, causal, ident = consts["scan_mask"], consts["causal"], consts["ident"]
    M = GPAIRS
    with Scope(nc, name) as s:
        ze = s.sb("z_e", [P, 2, M, T])
        z, e = ze[:, 0], ze[:, 1]
        lt = s.sb("ln_end", [P, 2, M, T])
        ln, to_end = lt[:, 0], lt[:, 1]
        b = s.sb("b", [P, M, T])
        eb = s.sb("exp_b", [P, M, T])
        enb = s.sb("exp_nb", [P, M, T])
        eke = s.sb("exp_end", [P, M, T])
        qd = s.sb("q_dec", [P, M, T])
        ki = s.sb("k_inv", [P, M, T])
        ke = s.sb("k_end", [P, M, T])
        keN = s.sb("k_end_rows", [P, NT, M, P])
        att = s.sb("att", [P, NT, GH, P])
        state = s.sb("state", [P, M, NCHUNK, GDV])
        o = s.sb("o", [P, NT, GH, GDV])
        sq = ze[:].rearrange("p a m t -> p (a m) t")
        ss = s.sb("ss", [P, NT * GH])
        root = s.sb("root", [P, NT * GH])
        sg = lt[:].rearrange("p a m t -> p (a m) t")
        tok = consts["tok"]
        zp = s.ps("psA", [P, 2, T])
        kt = s.ps("psT", [P, 2, T])
        kv = s.ps("psKV", [P, M, 2, NCHUNK // 2, GDV])
        z_done, zb, absd, ed, lnd, scand, expd, ended, eke_d = (s.sem(x) for x in (
            "z_done", "z_there", "abs", "exp", "ln", "scanned", "exps", "end_diff", "exp_end"))
        chain, ke_there, turned, rows, kv_done = (s.sem(x) for x in ("chain", "k_end", "turned", "rows", "kv_done"))
        dec_there, states, a_done, masked, o_done, o_taken, silu, ssd, rooted = (s.sem(x) for x in (
            "dec", "states", "a_done", "masked", "o_done", "o_taken", "silu", "ss", "rooted"))
        block = s.block()

        @block.tensor
        def _(pe):
            for m in range(M):
                last = nc.tensor.matmul(zp[:, m], w_alpha[:, m * P:(m + 1) * P], glrT[0:GRANK, :], start=True, stop=True)
            last.then_inc(z_done, 1)
            pe.wait_ge(ke_there, 1)
            for m in range(M):
                for t in range(NT):
                    last = nc.tensor.transpose(kt[:, m, t * P:(t + 1) * P], ke[:, m, t * P:(t + 1) * P], ident[:])
                last.then_inc(turned, 1)
            def scores(t):
                if t:
                    pe.wait_ge(masked, t)
                for h in range(GH):
                    m, r = h // 2, slice(GDK * (h % 2), GDK * (h % 2) + GDK)
                    last = nc.tensor.matmul(zp[:, h % 2, m * P:(m + 1) * P], ki[r, m, t * P:(t + 1) * P],
                                            qd[r, m, t * P:(t + 1) * P], start=True, stop=True)
                last.then_inc(a_done, 1)
            pe.wait_ge(dec_there, 1)
            scores(0)
            pe.wait_ge(rows, 1)
            for c in range(NCHUNK - 1):
                r, t = slice(GCHUNK * (c % 2), GCHUNK * (c % 2) + GCHUNK), c // 2
                for h in range(GH):
                    m, hh = h // 2, h % 2
                    last = nc.tensor.matmul(kv[GDK * hh:GDK * hh + GDK, m, c % 2, c // 2], keN[r, t, m, GDK * hh:GDK * hh + GDK],
                                            gv[r, t, h * GDV:(h + 1) * GDV], start=True, stop=True)
            last.then_inc(kv_done, 1)
            pe.wait_ge(states, 1)
            for t in range(NT):
                pe.wait_ge(masked, t + 1)
                if t:
                    pe.wait_ge(o_taken, t)
                for h in range(GH):
                    m, hh = h // 2, h % 2
                    r, cols = slice(GDK * hh, GDK * hh + GDK), slice(m * GDV, (m + 1) * GDV)
                    last = nc.tensor.matmul(kt[:, hh, cols], att[:, t, h], gv[:, t, h * GDV:(h + 1) * GDV],
                                            start=True, stop=False)
                    for c in (2 * t, 2 * t + 1):
                        half = GCHUNK * (c % 2)
                        last = nc.tensor.matmul(kt[half:half + GCHUNK, hh, cols], qd[r, m, c * GCHUNK:(c + 1) * GCHUNK],
                                                state[r, m, c], start=False, stop=True)
                last.then_inc(o_done, 1)
                if t + 1 < NT:
                    scores(t + 1)

        @block.scalar
        def _(act):
            act.wait_ge(zb, 1)
            nc.scalar.activation(e, z, ACT.Abs).then_inc(absd, 1)
            act.wait_ge(absd, 1)
            nc.scalar.activation(ln, e, ACT.Exp, scale=-1.0).then_inc(ed, 1)
            act.wait_ge(ed, 1)
            nc.scalar.activation(e, ln, ACT.Ln, bias=1.0).then_inc(lnd, 1)
            act.wait_ge(scand, M)
            nc.scalar.activation(eb[:], b[:], ACT.Exp, scale=1.0 / GATE_TAU).then_inc(expd, 1)
            nc.scalar.activation(enb[:], b[:], ACT.Exp, scale=-1.0 / GATE_TAU).then_inc(expd, 1)
            act.wait_ge(ended, 1)
            nc.scalar.activation(eke[:], to_end, ACT.Exp, scale=1.0 / GATE_TAU).then_inc(eke_d, 1)
            act.wait_ge(turned, M)
            nc.scalar.activation(keN[:].rearrange("p t m k -> p m t k"), kt[:].rearrange("p m (t k) -> p m t k", k=P),
                                 ACT.Copy).then_inc(rows, 1)
            nc.scalar.activation(sg, gg[:], ACT.Sigmoid).then_inc(silu, 1)
            for t in range(NT):
                act.wait_ge(o_done, t + 1)
                nc.scalar.activation(o[:, t].rearrange("p (m a) v -> p a m v", a=2),
                                     kt[:, :, 0:M * GDV].rearrange("p a (m v) -> p a m v", v=GDV), ACT.Copy).then_inc(o_taken, 1)
            act.wait_ge(ssd, 1)
            nc.scalar.activation(root[:], ss[:], ACT.Sqrt).then_inc(rooted, 1)

        @block.vector
        def _(dve):
            ch = Chain(dve, chain)
            link = ch.link
            nc.vector.memset(att[:], 0.0)
            nc.vector.memset(state[:, :, 0], 0.0)
            dve.wait_ge(z_done, 1)
            for m in range(M):
                last = nc.vector.tensor_scalar(z[:, m], zp[:, m], b_alpha[:, m:m + 1], None, ALU.add)
            last.then_inc(zb, 1)
            dve.wait_ge(lnd, 1)
            link(nc.vector.scalar_tensor_tensor(ln, z, 0.0, e, ALU.min, ALU.subtract))
            for m in range(M):
                nc.vector.tensor_tensor_scan(b[:, m], scan_mask[:], ln[:, m], 0.0, ALU.mult, ALU.add).then_inc(scand, 1)
            dve.wait_ge(scand, M)
            bc = b[:].rearrange("p m (n c) -> p (m n) c", c=GCHUNK)
            end = bc[:, :, GCHUNK - 1:GCHUNK].to_broadcast([P, M * NCHUNK, GCHUNK])
            nc.vector.tensor_tensor(to_end.rearrange("p m (n c) -> p (m n) c", c=GCHUNK), end, bc, ALU.subtract).then_inc(ended, 1)
            dve.wait_ge(expd, 2)
            nc.vector.scalar_tensor_tensor(qd[:], qkT[:, 0:M], float(GDK) ** -0.5, eb[:], ALU.mult, ALU.mult)
            nc.vector.tensor_tensor(ki[:], qkT[:, M:2 * M], enb[:], ALU.mult).then_inc(dec_there, 1)
            dve.wait_ge(eke_d, 1)
            nc.vector.tensor_tensor(ke[:], qkT[:, M:2 * M], eke[:], ALU.mult).then_inc(ke_there, 1)

            def mask(t):
                dve.wait_ge(a_done, t + 1)
                nc.vector.copy_predicated(att[:, t].rearrange("p (m a) i -> p a m i", a=2), causal[:].rearrange("p (a m i) -> p a m i", a=2, m=M),
                                          zp[:, :, 0:M * P].rearrange("p a (m i) -> p a m i", i=P)).then_inc(masked, 1)
            mask(0)
            dve.wait_ge(kv_done, 1)
            for c in range(NCHUNK - 1):
                for m in range(M):
                    new = kv[:, m, c % 2, c // 2]
                    if c == 0:
                        last = nc.vector.tensor_copy(state[:, m, 1], new)
                    else:
                        at = (c + 1) * GCHUNK - 1
                        last = nc.vector.scalar_tensor_tensor(state[:, m, c + 1], state[:, m, c], eb[:, m, at:at + 1], new,
                                                              ALU.mult, ALU.add)
                link(last)
            nc.vector.tensor_copy(tok[:], eb[:, 0, 0:1]).then_inc(states, 1)
            for t in range(1, NT):
                mask(t)
            dve.wait_ge(silu, 1)
            link(nc.vector.tensor_tensor(sg, sg, gg[:], ALU.mult))
            link(nc.vector.tensor_tensor(sg, sg, gain[:].unsqueeze(1).to_broadcast([P, NT, GV_W]), ALU.mult))
            for t in range(NT):
                dve.wait_ge(o_taken, t + 1)
                ot = o[:, t].rearrange("p h v -> p (h v)")
                link(nc.vector.tensor_tensor(sq[:, t], ot, ot, ALU.mult))
                link(nc.vector.tensor_reduce(ss[:, t * GH:(t + 1) * GH], sq[:, t].rearrange("p (h v) -> p h v", v=GDV), AX.X, ALU.add))
            nc.vector.tensor_scalar(ss[:], ss[:], 1.0 / GDV, EPS, ALU.mult, ALU.add).then_inc(ssd, 1)
            dve.wait_ge(rooted, 1)
            link(nc.vector.reciprocal(root[:], root[:]))
            r = root[:].unsqueeze(2).to_broadcast([P, NT * GH, GDV])
            of = o[:].rearrange("p t h v -> p (t h) v")
            link(nc.vector.tensor_tensor(of, of, r, ALU.mult))
            nc.vector.tensor_tensor(mixed[:, :, 0:GV_W], o[:].rearrange("p t h v -> p t (h v)"), sg, ALU.mult)


def attention_stage(nc, name, consts, bias, qkT, av, mixed):
    ident = consts["ident"]
    scale = float(AHD) ** -0.5
    A2 = AH * AHD // P
    units = [(t, h) for t in range(NT) for h in range(AH)]
    with Scope(nc, name) as s:
        sc = s.sb("scores", [P, 2, T])
        mx = s.sb("mx", [P, NT * AH])
        nb = s.sb("nb", [P, NT * AH])
        pr = s.sb("probs", [P, 2, T])
        den = s.sb("den", [P, NT * AH])
        rden = s.sb("rden", [P, NT * AH])
        pT = s.sb("probsT", [P, 2, T])
        ps_s = s.ps("ps_s", [P, 2, T])
        ps_t = s.ps("ps_t", [P, 2, T])
        ps_o = s.ps("ps_o", [P, 2, T])
        qk_done, biased, neg, prob, turned, kept, o_done, recip, o_taken = (s.sem(x) for x in (
            "qk_done", "biased", "neg", "prob", "turned", "kept", "o_done", "recip", "o_taken"))
        block = s.block()

        @block.tensor
        def _(pe):
            def qk(u):
                t, h = units[u]
                r = slice(AHD * (h % 2), AHD * (h % 2) + AHD)
                wait(pe, biased, u - 1)
                nc.tensor.matmul(ps_s[:, u % 2, 0:(t + 1) * P], qkT[r, h // 2, t * P:(t + 1) * P],
                                 qkT[r, A2 + h // 2, 0:(t + 1) * P], start=True, stop=True).then_inc(qk_done, 1)

            def turn(u):
                t, h = units[u]
                pe.wait_ge(prob, u + 1)
                wait(pe, kept, u - 1)
                for k in range(t + 1):
                    last = nc.tensor.transpose(ps_t[:, u % 2, k * P:(k + 1) * P], pr[:, u % 2, k * P:(k + 1) * P], ident[:])
                last.then_inc(turned, 1)

            def pv(u):
                t, h = units[u]
                pe.wait_ge(kept, u + 1)
                wait(pe, o_taken, u - 1)
                for k in range(t + 1):
                    last = nc.tensor.matmul(ps_o[:, u % 2, 0:AHD], pT[:, u % 2, k * P:(k + 1) * P],
                                            av[:, k, h * AHD:(h + 1) * AHD], start=(k == 0), stop=(k == t))
                last.then_inc(o_done, 1)

            n = len(units)
            for u in range(n + 2):
                if u < n:
                    qk(u)
                if 1 <= u <= n:
                    turn(u - 1)
                if u >= 2:
                    pv(u - 2)

        @block.scalar
        def _(act):
            for u, (t, h) in enumerate(units):
                w = (t + 1) * P
                act.wait_ge(neg, u + 1)
                wait(act, turned, u - 1)
                nc.scalar.activation(pr[:, u % 2, 0:w], sc[:, u % 2, 0:w], ACT.Exp, bias=nb[:, u:u + 1], scale=scale,
                                     accum_out=den[:, u:u + 1]).then_inc(prob, 1)
                act.wait_ge(turned, u + 1)
                wait(act, o_done, u - 1)
                nc.scalar.activation(pT[:, u % 2, 0:w], ps_t[:, u % 2, 0:w], ACT.Copy).then_inc(kept, 1)

        @block.vector
        def _(dve):
            def finish(u):
                t, h = units[u]
                dve.wait_ge(prob, u + 1)
                nc.vector.reciprocal(rden[:, u:u + 1], den[:, u:u + 1]).then_inc(recip, 1)
                dve.wait_ge(recip, u + 1)
                dve.wait_ge(o_done, u + 1)
                nc.vector.tensor_scalar(mixed[:, t, GV_W + h * AHD:GV_W + (h + 1) * AHD], ps_o[:, u % 2, 0:AHD],
                                        rden[:, u:u + 1], None, ALU.mult).then_inc(o_taken, 1)

            for u, (t, h) in enumerate(units):
                w = (t + 1) * P
                dve.wait_ge(qk_done, u + 1)
                wait(dve, prob, u - 1)
                nc.vector.tensor_tensor_reduce(out=sc[:, u % 2, 0:w], in0=ps_s[:, u % 2, 0:w], in1=bias[:, h, T - w:T],
                                               scale=1.0, scalar=NEG, op0=ALU.add, op1=ALU.max,
                                               accum_out=mx[:, u:u + 1]).then_inc(biased, 1)
                dve.wait_ge(biased, u + 1)
                nc.vector.tensor_scalar(nb[:, u:u + 1], mx[:, u:u + 1], -scale, None, ALU.mult).then_inc(neg, 1)
                if u >= 3:
                    finish(u - 3)
            for u in range(len(units) - 3, len(units)):
                finish(u)


class Final:

    def __init__(self, nc, s, resid, final_norm, out, xn, gain, after):
        self.nc, self.resid, self.final_norm, self.out, self.xn, self.gain = nc, resid, final_norm, out, xn, gain
        self.after = after
        self.ss, self.rs = s.sb("f_ss", [P, NT]), s.sb("f_rs", [P, NT])
        self.gain_in, self.squared, self.mean, self.rooted, self.chain, self.there, self.stored = (s.sem(f"f_{x}") for x in (
            "gain_in", "squared", "mean", "rooted", "chain", "there", "stored"))

    def sp(self, sp):
        sp.wait_ge(*self.after)
        sp.dma_start(self.gain, self.final_norm.partition_broadcast(P)).then_inc(self.gain_in, 16)
        rows = self.out.rearrange("(t p) d -> p t d", p=P)
        for t in range(NT):
            sp.wait_ge(self.there, t + 1)
            sp.dma_start(rows[:, t], self.xn[:, t]).then_inc(self.stored, 16)
        sp.wait_ge(self.stored, NT * 16)

    def act(self, act):
        sem, count = self.after
        for t in range(NT):
            act.wait_ge(sem, count - NT + t + 1)
            self.nc.scalar.activation(self.xn[:, t], self.resid[:, t], ACT.Square, accum_out=self.ss[:, t:t + 1]).then_inc(self.squared, 1)
        act.wait_ge(self.mean, 1)
        self.nc.scalar.activation(self.rs[:], self.ss[:], ACT.Sqrt).then_inc(self.rooted, 1)

    def dve(self, dve):
        nc, link = self.nc, Chain(dve, self.chain).link
        dve.wait_ge(self.squared, NT)
        nc.vector.tensor_scalar(self.ss[:], self.ss[:], 1.0 / D, EPS, ALU.mult, ALU.add).then_inc(self.mean, 1)
        dve.wait_ge(self.rooted, 1)
        link(nc.vector.reciprocal(self.rs[:], self.rs[:]))
        dve.wait_ge(self.gain_in, 16)
        for t in range(NT):
            nc.vector.scalar_tensor_tensor(self.xn[:, t], self.resid[:, t], self.rs[:, t:t + 1], self.gain, ALU.mult,
                                           ALU.mult).then_inc(self.there, 1)


class LowRank:

    def __init__(self, nc, s, dram, bank, xh, xl, dest):
        self.nc, self.dram, self.ps, self.xh, self.xl, self.dest = nc, dram, bank, xh, xl, dest
        self.raw, self.wh, self.wl = s.sb("r_raw", [P, KD, P]), s.sb("r_hi", [P, KD, P], F32R), s.sb("r_lo", [P, KD, P], F32R)
        self.loaded, self.high, self.low, self.done = (s.sem(f"rank_{x}") for x in ("loaded", "high", "low", "done"))

    def sp(self, sp):
        sp.dma_start(self.raw[:].rearrange("p k c -> p (k c)"), self.dram).then_inc(self.loaded, 16)

    def act(self, act):
        act.wait_ge(self.loaded, 16)
        self.nc.scalar.activation(self.wh[:], self.raw[:], ACT.Copy).then_inc(self.high, 1)

    def dve_low(self, dve):
        dve.wait_ge(self.high, 1)
        self.nc.vector.tensor_tensor(self.wl[:], self.raw[:], self.wh[:].bitcast(F32), ALU.subtract).then_inc(self.low, 1)

    def dve_take(self, dve):
        dve.wait_ge(self.done, 1)
        self.nc.vector.tensor_copy(self.dest[:], self.ps[:, 4])

    def pe(self, pe):
        pe.wait_ge(self.low, 1)
        for d in range(KD):
            last = three_pass(self.nc, self.ps[:, 4], self.wh[:, d], self.wl[:, d], self.xh[:, d], self.xl[:, d], d == 0, d == KD - 1)
        last.then_inc(self.done, 1)


def trunk(nc, A, out):
    Scope.HELD.clear()
    hT = nc.dram_tensor("hidden_scratch", (PAIRS, P, 2 * T), F32).ap()
    gT = nc.dram_tensor("gate_scratch", (T // TB, P, NKEYS * TB), F32).ap()
    with Scope(nc, "main") as s:
        resid = s.sb("resid", [P, NT, D])
        gains = s.sb("gains", [P, 4, KD])
        ident = s.sb("ident", [P, P])
        iota = s.sb("iota", [P, P])
        tok = s.sb("tok", [P, 1])
        xh = s.sb("x_hi", [P, KD, T], F32R)
        xl = s.sb("x_lo", [P, KD, T], F32R)
        consts = {"ident": ident, "iota": iota, "tok": tok}

        with Scope(nc, "l0") as m:
            byc = m.sb("by_column", [P, 12, T])
            byr = m.sb("by_row", [P, NT, 3 * T])
            glrT = m.sb("gate_rankT", [P, T])
            with Scope(nc, "in0") as b:
                w = Stream(nc, b)
                bank = b.ps("bank", [P, 8, T])
                xn = b.sb("xn", [P, NT, D])
                loaded = b.sem("loaded")
                norm = Norm(nc, b, "norm", resid, gains[:, 0], ident, bank, xn, xh, xl, (loaded, 64))
                cols = Project(nc, b, "cols", w, 0, A["w_ab_T"], 6, bank, xh, xl, norm.ready, byc, True)
                rows = Project(nc, b, "rows", w, 6, A["w_ab_N"], 6, bank, xh, xl, None, byr, False)
                rank = LowRank(nc, b, A["w_glr"], bank, xh, xl, glrT)
                block = b.block()

                @block.sync
                def _(sp):
                    for dst, src in ((resid[:], A["x"].rearrange("(t p) d -> p t d", p=P)), (gains[:], A["gains"]), (ident[:], A["ident"]),
                                     (iota[:], A["iota"].partition_broadcast(P))):
                        sp.dma_start(dst, src).then_inc(loaded, 16)
                    rank.sp(sp)
                    cols.sp(sp)
                    rows.sp(sp)

                @block.gpsimd
                def _(pool):
                    w.all_low(pool, 12)

                @block.scalar
                def _(act):
                    norm.act(act)
                    rank.act(act)
                    cols.act(act)
                    rows.act(act)

                @block.vector
                def _(dve):
                    norm.dve(dve)
                    rank.dve_low(dve)
                    cols.dve(dve)
                    rank.dve_take(dve)
                    rows.dve(dve)

                @block.tensor
                def _(pe):
                    pe.wait_ge(loaded, 64)
                    norm.pe(pe)
                    cols.pe(pe)
                    rank.pe(pe)
                    pe.wait_ge(cols.taken, 6)
                    rows.pe(pe)

            mixed = m.sb("mixed", [P, NT, D])
            with Scope(nc, "gla_c") as g:
                scan_mask, causal = g.sb("scan_mask", [P, T]), g.sb("causal", [P, T], I32)
                w_alpha, b_alpha, gain = g.sb("w_alpha", [GRANK, GH * GDK]), g.sb("b_alpha", [P, GPAIRS]), g.sb("gain", [P, GV_W])
                consts |= {"scan_mask": scan_mask, "causal": causal}
                with Scope(nc, "gla_l") as l:
                    loaded = l.sem("loaded")
                    block = l.block()

                    @block.sync
                    def _(sp):
                        loads = ((scan_mask[:], A["scan_mask"].partition_broadcast(P)), (causal[:], A["causal"]), (w_alpha[:], A["w_alpha"]),
                                 (b_alpha[:], A["b_alpha"]), (gain[:], A["head_gain"].partition_broadcast(P)))
                        for dst, src in loads:
                            sp.dma_start(dst, src).then_inc(loaded, 16)
                        sp.wait_ge(loaded, len(loads) * 16)
                gla_stage(nc, "gla", consts, byc[:, 0:4], byr[:, :, 0:T], byr[:, :, T:2 * T], glrT, w_alpha, b_alpha, gain, mixed)
            with Scope(nc, "att_c") as g:
                bias = g.sb("bias", [P, AH, T])
                with Scope(nc, "att_l") as l:
                    loaded = l.sem("loaded")
                    block = l.block()

                    @block.sync
                    def _(sp):
                        sp.dma_start(bias[:], A["att_bias"]).then_inc(loaded, 16)
                        sp.wait_ge(loaded, 16)
                attention_stage(nc, "att", consts, bias, byc[:, 4:12], byr[:, :, 2 * T:3 * T], mixed)
            with Scope(nc, "mixT") as b:
                bank = b.ps("bank", [P, 8, T])
                turn = SplitRows(nc, b, "turn", mixed, ident, bank, xh, xl)
                block = b.block()
                block.tensor(turn.pe)
                block.scalar(turn.act)
                block.vector(turn.dve)
        expert_layer(nc, A, 0, "w_out0", resid, gains, consts, hT, gT, xh, xl, None)
        Scope.reset(nc)
        expert_layer(nc, A, 1, "w_c_out", resid, gains, consts, hT, gT, xh, xl, out)


def expert_layer(nc, A, layer, w_out, resid, gains, consts, hT, gT, xh, xl, out):
    ident = consts["ident"]
    recurrent = layer == 1
    with Scope(nc, f"l{layer}x") as s:
        w = Stream(nc, s)
        bank = s.ps("bank", [P, 8, T])
        room = Room(nc, s, ROOM)
        part = room.part
        scores = part("scores", 0, [P, NT, 2 * PH, NKEYS])
        gin = part("g_in", 0, [P, 2, T // TB, 4, TB])
        hin = part("h_in", 4096, [P, 4, 2, T])
        gst = part("g_out", 8192, [P, 2, NKEYS, TB])
        keys = part("keys", 8192, [P, 2 * PH * NKEYS])
        q = part("q", 8192 + 2048, [P, 2, 2, T])
        xn = part("xn", 8192 + 4096, [P, NT, D])
        a = part("a", 8192, [P, 4, T])
        ah = part("a_hi", 8192 + 2048, [P, 4, T], F32R)
        al = part("a_lo", 8192 + 4096, [P, 4, T], F32R)
        nq = D // BC
        if recurrent:
            gxT = part("gate_x", 0, [P, 2 * RT, T])
            xc = part("conv", 8192, [P, RT, T])
            ig = part("i_gate", 12288, [P, RT, T])
            av = part("a_gate", 16384, [P, RT, T])
            rg = part("r_gate", 20480, [P, RT, T])
            yl = part("y_lo", 8192, [P, RT, T], F32R)
            yh = part("y_hi", 20480, [P, RT, T], F32R)
            xn_in = part("xn_in", 0, [P, NT, D])
            norm_in = Norm(nc, s, "norm_in", resid, gains[:, 1], ident, bank, xn_in, xh, xl)
            wr, wi = part("w_rgate", 24576, [P, RT, P]), part("w_igate", 25600, [P, RT, P])
            rec = Recurrent(nc, s, w, 0, A, bank, xh, xl, norm_in.ready, gxT, xc, rg, ig, av, yh, yl, wr, wi)
            base = Recurrent.BLOCKS
            proj = Project(nc, s, "out", w, base, A[w_out], nq, bank, yh, yl, rec.ready, resid, False, add=True)
        else:
            base = 0
            proj = Project(nc, s, "out", w, base, A[w_out], nq, bank, xh, xl, None, resid, False, add=True)
        norm = Norm(nc, s, "norm", resid, gains[:, 2 + layer], ident, bank, xn, xh, xl, (proj.taken, nq))
        query = Queries(nc, s, w, base + nq, A["w_query"][layer], A["keysT"][layer], bank, xh, xl, norm.ready, keys, q, scores)
        up = Up(nc, s, w, base + nq + PH, A["uT"][layer], hT, gT, consts, bank, xh, xl, scores, gst, room)
        down = Down(nc, s, w, base + nq + PH + PAIRS, A["v"][layer], up, hT, gT, bank, resid, hin, gin, a, ah, al)
        final = None
        if out is not None:
            gain = part("f_gain", 8192, [P, D])
            xf = part("f_xn", 0, [P, NT, D])
            final = Final(nc, s, resid, A["final_norm"], out, xf, gain[:], (down.added, NT))
        block = s.block()

        @block.sync
        def _(sp):
            if recurrent:
                rec.sp(sp)
            proj.sp(sp)
            query.sp(sp, (proj.taken, nq))
            up.sp(sp)
            down.sp(sp)
            if final:
                final.sp(sp)

        @block.gpsimd
        def _(pool):
            w.all_low(pool, base + nq + PH + 2 * PAIRS)

        @block.scalar
        def _(act):
            if recurrent:
                norm_in.act(act)
                rec.act(act)
            proj.act(act)
            norm.act(act)
            query.act(act)
            up.act(act)
            down.act(act)
            if final:
                final.act(act)

        @block.vector
        def _(dve):
            if recurrent:
                norm_in.dve(dve)
                rec.dve(dve)
            proj.dve(dve)
            norm.dve(dve)
            query.dve(dve)
            up.dve(dve)
            down.dve(dve)
            if final:
                final.dve(dve)

        @block.tensor
        def _(pe):
            if recurrent:
                norm_in.pe(pe)
                rec.pe(pe)
            proj.pe(pe)
            norm.pe(pe)
            query.pe(pe)
            up.pe(pe, lambda: query.pe_last(pe))
            down.pe(pe)


def kernel(**inputs):
    import concourse.bacc as bacc
    from concourse.bass_utils import run_bass_kernel_spmd

    x = {k: np.asarray(v) for k, v in inputs.items()}

    def blocks(w, starts, width=BC):
        return np.ascontiguousarray(np.stack([w[:, c:c + width].reshape(KD, P, width).transpose(1, 0, 2).reshape(P, KD * width)
                                              for c in starts]))

    def columns(v):
        return np.ascontiguousarray(v.reshape(-1, P).T)

    qk, vw, aw = GH * GDK, GV_W, AH * AHD
    at_gv, at_gg, at_glr = 2 * qk, 2 * qk + vw, 2 * qk + 2 * vw
    at_aq = at_glr + GRANK
    at_ak, at_av = at_aq + aw, at_aq + 2 * aw
    w_in = x["ab_w_in"][0]
    wide = range(0, D, BC)

    delta = (T - P) + np.arange(P)[:, None] - np.arange(T)[None, :]
    count = np.zeros(delta.shape)
    for window, dil in BRANCHES:
        count += (delta >= 0) & (delta % dil == 0) & (delta <= window)
    slopes = 2.0 ** (-8.0 * np.arange(1, AH + 1) / AH)
    with np.errstate(divide="ignore"):
        penalty = np.where(count > 0, np.log(np.maximum(count, 1)), -1e30)
    att_bias = (math.sqrt(AHD) * (penalty[:, None, :] - slopes[None, :, None] * delta[:, None, :])).astype(np.float32)
    j, i = np.arange(P)[:, None], np.arange(P)[None, :]
    causal = np.tile(((j <= i) & (j // GCHUNK == i // GCHUNK)).astype(np.int32), (1, GH))

    arrays = {
        "x": x["x"].reshape(T, D),
        "gains": np.stack([columns(x[n][k]) for n in ("mix_norm", "ffn_norm") for k in range(2)], axis=1),
        "ident": np.eye(P, dtype=np.float32),
        "iota": np.arange(P, dtype=np.float32),
        "scan_mask": (np.arange(T) % GCHUNK != 0).astype(np.float32),
        "causal": causal,
        "att_bias": att_bias,
        "w_glr": blocks(w_in, [at_glr], P)[0],
        "w_ab_T": blocks(w_in, [0, qk, at_aq, at_aq + BC, at_ak, at_ak + BC]),
        "w_ab_N": blocks(w_in, [at_gv, at_gv + BC, at_gg, at_gg + BC, at_av, at_av + BC]),
        "w_alpha": x["gla_w_alpha"][0],
        "b_alpha": columns(x["gla_b_alpha"][0]),
        "head_gain": x["gla_head_gain"][0],
        "w_out0": blocks(x["ab_w_out"][0], wide),
        "w_c_in": blocks(x["c_w_in"][0], [*range(D, 2 * D, BC), *range(0, D, BC)]),
        "conv_w": x["c_conv_w"][0].reshape(CONV, RT, P).transpose(2, 1, 0),
        "conv_b": columns(x["c_conv_b"][0]),
        "w_rgate": x["c_w_rgate"][0].transpose(1, 0, 2),
        "w_igate": x["c_w_igate"][0].transpose(1, 0, 2),
        "b_rgate": columns(x["c_b_rgate"][0]),
        "b_igate": columns(x["c_b_igate"][0]),
        "lam": columns(x["c_lambda"][0]),
        "w_c_out": blocks(x["c_w_out"][0], wide),
        "w_query": np.stack([blocks(x["peer_w_query"][k], range(0, 2 * PH * P, BC)) for k in range(2)]),
        "keysT": x["peer_sub_keys"].transpose(0, 4, 1, 2, 3).reshape(2, P, 2 * PH * NKEYS),
        "uT": x["peer_u"].reshape(2, NCH // 2, 2, P, KD, P).transpose(0, 1, 5, 2, 4, 3).reshape(2, NCH // 2, P, 2 * KD * P),
        "v": x["peer_v"],
        "final_norm": x["final_norm"],
    }
    nc = bacc.Bacc("TRN2", target_bir_lowering=False, num_devices=1)
    feed, A = {}, {}
    for name, a in arrays.items():
        feed[f"in_{name}"] = np.ascontiguousarray(a)
        A[name] = nc.dram_tensor(f"in_{name}", a.shape, mybir.dt.from_np(a.dtype), kind="ExternalInput").ap()
    out = nc.dram_tensor("out_0", (T, D), F32, kind="ExternalOutput").ap()
    trunk(nc, A, out)
    r = run_bass_kernel_spmd(nc, [feed], core_ids=[0])
    return r.results[0]["out_0"].reshape(inputs["x"].shape)
```
